# Optimizing a Trainium2 kernel written in Bass

```python
import jax, jax.numpy as jnp
from jax import lax
import numpy as np

'''Two layers of a chunk-causal hybrid encoder trunk with adaLN conditioning.

Each layer: macaron half-step SwiGLU FFN -> parallel-branch token mixing
(sliding-window GQA with sinks | multi-scale pooling | Conformer conv module |
short gated conv), merged by per-channel sigmoid gates and one output
projection -> macaron half-step SwiGLU FFN. Every sub-layer: pre-RMSNorm,
adaLN shift/scale from c, adaLN gate on the residual update.

Inputs: x (BATCH, SEQ, D_MODEL) f32, c (BATCH, D_MODEL) f32,
positions (BATCH, SEQ) int32 absolute stream positions (used by rotary).
Output: (BATCH, SEQ, D_MODEL).
'''

D_MODEL = 1024
BATCH = 1
SEQ = 512
DEPTH = 2

CHUNK = 64
EPS = 1e-6
ATTN_HEADS = 8
ATTN_KV_HEADS = 2
HEAD_DIM = 64
WINDOW = 128
WINDOW_CHUNKS = WINDOW // CHUNK
ROPE_THETA = 10000.0
Q_WIDTH = ATTN_HEADS * HEAD_DIM
KV_WIDTH = ATTN_KV_HEADS * HEAD_DIM
POOL_WINDOWS = (2, 4, 8, 16)
POOL_GROUP = 128
POOL_WIDTH = len(POOL_WINDOWS) * POOL_GROUP
POOL_OUT_GROUP = D_MODEL // len(POOL_WINDOWS)
CONV_WIDTH = 512
CONV_KERNEL = 31
SC_WIDTH = 512
SC_KERNEL = 3
N_BRANCHES = 4
N_MOD = 9
D_FF = 2816
IN_WIDTH = Q_WIDTH + 2 * KV_WIDTH + POOL_WIDTH + 2 * CONV_WIDTH + 3 * SC_WIDTH

kernel_name = 'hybrid_chunk_causal_block'

def rmsnorm(x, g):
    x32 = x.astype(jnp.float32)
    y = x32 * lax.rsqrt(jnp.mean(x32 * x32, axis=-1, keepdims=True) + EPS)
    return (y * g.astype(jnp.float32)).astype(x.dtype)

def layernorm(x, g, b):
    x32 = x.astype(jnp.float32)
    mu = jnp.mean(x32, axis=-1, keepdims=True)
    xc = x32 - mu
    y = xc * lax.rsqrt(jnp.mean(xc * xc, axis=-1, keepdims=True) + EPS)
    return (y * g.astype(jnp.float32) + b.astype(jnp.float32)).astype(x.dtype)

def modulate(h, shift, scale):
    return h * (1.0 + scale) + shift

def swiglu(h, wi, wo):
    gate, up = jnp.split(h @ wi, 2, axis=-1)
    return (jax.nn.silu(gate) * up) @ wo

def rope_tables(positions):
    inv = (ROPE_THETA ** (-np.arange(0, HEAD_DIM, 2, dtype=np.float32) / HEAD_DIM)).astype(np.float32)
    ang = positions.astype(jnp.float32)[..., None] * inv
    return jnp.cos(ang)[:, :, None, :], jnp.sin(ang)[:, :, None, :]

def apply_rope(x, cos, sin):
    x32 = x.astype(jnp.float32)
    x1, x2 = jnp.split(x32, 2, axis=-1)
    out = jnp.concatenate([x1 * cos - x2 * sin, x2 * cos + x1 * sin], axis=-1)
    return out.astype(x.dtype)

def causal_dwconv(x, w):
    k = w.shape[0]
    return lax.conv_general_dilated(
        x, w[:, None, :].astype(x.dtype), window_strides=(1,), padding=[(k - 1, 0)],
        dimension_numbers=('NWC', 'WIO', 'NWC'), feature_group_count=x.shape[-1])

def swa_sink_attention(q, k, v, sinks):
    b, s, hq, hd = q.shape
    hkv = k.shape[2]
    g = hq // hkv
    n_chunks = s // CHUNK
    qb = q.reshape(b, n_chunks, CHUNK, hkv, g, hd)
    pad = jnp.zeros((b, (WINDOW_CHUNKS - 1) * CHUNK, hkv, hd), k.dtype)
    kp = jnp.concatenate([pad, k], axis=1).reshape(b, n_chunks + WINDOW_CHUNKS - 1, CHUNK, hkv, hd)
    vp = jnp.concatenate([pad, v], axis=1).reshape(b, n_chunks + WINDOW_CHUNKS - 1, CHUNK, hkv, hd)
    kb = jnp.concatenate([kp[:, j:j + n_chunks] for j in range(WINDOW_CHUNKS)], axis=2)
    vb = jnp.concatenate([vp[:, j:j + n_chunks] for j in range(WINDOW_CHUNKS)], axis=2)
    scores = jnp.einsum('bcqhgd,bckhd->bchgqk', qb, kb).astype(jnp.float32) * (hd ** -0.5)
    key_chunk = np.arange(n_chunks)[:, None] - (WINDOW_CHUNKS - 1) + np.arange(WINDOW_CHUNKS)[None, :]
    valid = np.repeat(key_chunk >= 0, CHUNK, axis=1)
    scores = jnp.where(valid[None, :, None, None, None, :], scores, -1e30)
    sink = sinks.astype(jnp.float32).reshape(1, 1, hkv, g, 1, 1)
    m = jnp.maximum(jnp.max(scores, axis=-1, keepdims=True), sink)
    p = jnp.exp(scores - m)
    probs = p / (jnp.sum(p, axis=-1, keepdims=True) + jnp.exp(sink - m))
    out = jnp.einsum('bchgqk,bckhd->bcqhgd', probs.astype(v.dtype), vb)
    return out.reshape(b, s, hq * hd)

def multiscale_pool(u, pool_w):
    b, s, _ = u.shape
    t = np.arange(1, s + 1, dtype=np.float32)
    outs = []
    for gi, w in enumerate(POOL_WINDOWS):
        ug = u[..., gi * POOL_GROUP:(gi + 1) * POOL_GROUP].astype(jnp.float32)
        cs = jnp.concatenate([jnp.zeros((b, w, POOL_GROUP), jnp.float32), jnp.cumsum(ug, axis=1)], axis=1)
        win_sum = cs[:, w:] - cs[:, :-w]
        mean = win_sum / np.minimum(t, np.float32(w))[None, :, None]
        outs.append((mean - ug).astype(u.dtype) @ pool_w[gi])
    return jnp.concatenate(outs, axis=-1)

def conformer_conv(u, dw, db, ln_g, ln_b, wo):
    a, gate = jnp.split(u, 2, axis=-1)
    z = a * jax.nn.sigmoid(gate)
    z = causal_dwconv(z, dw) + db
    z = layernorm(z, ln_g, ln_b)
    return jax.nn.silu(z) @ wo

def hybrid_mixer(h, cos, sin, w_in, w_gate, b_gate, q_norm, k_norm, attn_sinks, attn_wo,
                 pool_w, pool_scale, conv_dw, conv_db, conv_ln_g, conv_ln_b, conv_wo,
                 sc_w, sc_wo, w_o):
    b, s, _ = h.shape
    o1 = Q_WIDTH
    o2 = o1 + KV_WIDTH
    o3 = o2 + KV_WIDTH
    o4 = o3 + POOL_WIDTH
    o5 = o4 + 2 * CONV_WIDTH
    o6 = o5 + SC_WIDTH
    o7 = o6 + SC_WIDTH
    proj = h @ w_in
    q, k, v, u_pool, u_conv, sc_b, sc_c, sc_x = jnp.split(proj, [o1, o2, o3, o4, o5, o6, o7], axis=-1)
    q = apply_rope(rmsnorm(q.reshape(b, s, ATTN_HEADS, HEAD_DIM), q_norm), cos, sin)
    k = apply_rope(rmsnorm(k.reshape(b, s, ATTN_KV_HEADS, HEAD_DIM), k_norm), cos, sin)
    v = v.reshape(b, s, ATTN_KV_HEADS, HEAD_DIM)
    y_a = swa_sink_attention(q, k, v, attn_sinks) @ attn_wo
    y_b = multiscale_pool(u_pool, pool_w) * pool_scale
    y_c = conformer_conv(u_conv, conv_dw, conv_db, conv_ln_g, conv_ln_b, conv_wo)
    y_d = (sc_b * causal_dwconv(sc_c * sc_x, sc_w)) @ sc_wo
    gates = jax.nn.sigmoid(h @ w_gate + b_gate).reshape(b, s, N_BRANCHES, D_MODEL)
    merged = (gates[:, :, 0] * y_a + gates[:, :, 1] * y_b
              + gates[:, :, 2] * y_c + gates[:, :, 3] * y_d)
    return merged @ w_o

def setup_inputs(seed: int = 0) -> dict:
    key = jax.random.key(seed)
    ks = list(jax.random.split(key, 40))
    nxt = iter(ks)

    def nrm(shape, scale):
        return jax.random.normal(next(nxt), shape, jnp.float32) * scale

    def gain(shape):
        return 1.0 + nrm(shape, 0.1)

    L = DEPTH
    x = nrm((BATCH, SEQ, D_MODEL), 1.0)
    c = nrm((BATCH, D_MODEL), 1.0)
    start = jax.random.randint(next(nxt), (BATCH, 1), 0, 1024, dtype=jnp.int32)
    positions = start + jnp.arange(SEQ, dtype=jnp.int32)[None, :]
    return {
        'x': x,
        'c': c,
        'positions': positions,
        'ada_w': nrm((L, D_MODEL, N_MOD * D_MODEL), 0.5 * D_MODEL ** -0.5),
        'ada_b': nrm((L, N_MOD * D_MODEL), 0.01),
        'ffn1_norm': gain((L, D_MODEL)),
        'ffn1_wi': nrm((L, D_MODEL, 2 * D_FF), D_MODEL ** -0.5),
        'ffn1_wo': nrm((L, D_FF, D_MODEL), D_FF ** -0.5),
        'mix_norm': gain((L, D_MODEL)),
        'w_in': nrm((L, D_MODEL, IN_WIDTH), D_MODEL ** -0.5),
        'w_gate': nrm((L, D_MODEL, N_BRANCHES * D_MODEL), D_MODEL ** -0.5),
        'b_gate': nrm((L, N_BRANCHES * D_MODEL), 0.01),
        'q_norm': gain((L, HEAD_DIM)),
        'k_norm': gain((L, HEAD_DIM)),
        'attn_sinks': nrm((L, ATTN_HEADS), 0.5),
        'attn_wo': nrm((L, Q_WIDTH, D_MODEL), Q_WIDTH ** -0.5),
        'pool_w': nrm((L, len(POOL_WINDOWS), POOL_GROUP, POOL_OUT_GROUP), POOL_GROUP ** -0.5),
        'pool_scale': gain((L, D_MODEL)),
        'conv_dw': nrm((L, CONV_KERNEL, CONV_WIDTH), CONV_KERNEL ** -0.5),
        'conv_db': nrm((L, CONV_WIDTH), 0.01),
        'conv_ln_g': gain((L, CONV_WIDTH)),
        'conv_ln_b': nrm((L, CONV_WIDTH), 0.01),
        'conv_wo': nrm((L, CONV_WIDTH, D_MODEL), CONV_WIDTH ** -0.5),
        'sc_w': nrm((L, SC_KERNEL, SC_WIDTH), SC_KERNEL ** -0.5),
        'sc_wo': nrm((L, SC_WIDTH, D_MODEL), SC_WIDTH ** -0.5),
        'w_o': nrm((L, D_MODEL, D_MODEL), D_MODEL ** -0.5),
        'ffn2_norm': gain((L, D_MODEL)),
        'ffn2_wi': nrm((L, D_MODEL, 2 * D_FF), D_MODEL ** -0.5),
        'ffn2_wo': nrm((L, D_FF, D_MODEL), D_FF ** -0.5),
    }

def reference(x, c, positions, ada_w, ada_b, ffn1_norm, ffn1_wi, ffn1_wo, mix_norm, w_in,
              w_gate, b_gate, q_norm, k_norm, attn_sinks, attn_wo, pool_w, pool_scale,
              conv_dw, conv_db, conv_ln_g, conv_ln_b, conv_wo, sc_w, sc_wo, w_o,
              ffn2_norm, ffn2_wi, ffn2_wo):
    cos, sin = rope_tables(positions)
    cond = jax.nn.silu(c)
    b = x.shape[0]
    for l in range(DEPTH):
        mod = (cond @ ada_w[l] + ada_b[l]).reshape(b, N_MOD, 1, D_MODEL)
        sh1, sc1, g1 = mod[:, 0], mod[:, 1], mod[:, 2]
        sh2, sc2, g2 = mod[:, 3], mod[:, 4], mod[:, 5]
        sh3, sc3, g3 = mod[:, 6], mod[:, 7], mod[:, 8]
        h = modulate(rmsnorm(x, ffn1_norm[l]), sh1, sc1)
        x = x + 0.5 * g1 * swiglu(h, ffn1_wi[l], ffn1_wo[l])
        h = modulate(rmsnorm(x, mix_norm[l]), sh2, sc2)
        y = hybrid_mixer(h, cos, sin, w_in[l], w_gate[l], b_gate[l], q_norm[l], k_norm[l],
                         attn_sinks[l], attn_wo[l], pool_w[l], pool_scale[l], conv_dw[l],
                         conv_db[l], conv_ln_g[l], conv_ln_b[l], conv_wo[l], sc_w[l],
                         sc_wo[l], w_o[l])
        x = x + g2 * y
        h = modulate(rmsnorm(x, ffn2_norm[l]), sh3, sc3)
        x = x + 0.5 * g3 * swiglu(h, ffn2_wi[l], ffn2_wo[l])
    return x


_drawn_inputs = setup_inputs


def setup_inputs(seed=0):
    import zlib

    import numpy as np

    out = dict(_drawn_inputs(seed))
    spreads = {}
    factors = {'ada_b': 3.196,
     'b_gate': 8.0,
     'q_norm': 8.0,
     'k_norm': 8.0,
     'attn_sinks': 8.0,
     'pool_scale': 2.7,
     'conv_db': 8.0,
     'conv_ln_g': 3.631,
     'conv_ln_b': 27.383,
     'ffn2_norm': 2.834}
    for name, (base, spread) in spreads.items():
        noise = np.random.default_rng([zlib.crc32(name.encode()), seed]).standard_normal(out[name].shape)
        drawn = base * np.exp(spread * noise) if base else spread * noise
        out[name] = __import__('jax').numpy.asarray(drawn.astype(out[name].dtype))
    for name, factor in factors.items():
        out[name] = (out[name] * factor).astype(out[name].dtype)
    return out
```

```python
from contextlib import ExitStack

import numpy as np
import concourse.bass as bass
from concourse import mybir

F32 = mybir.dt.float32
F32R = mybir.dt.float32r
I32 = mybir.dt.int32
ACT = mybir.ActivationFunctionType
ALU = mybir.AluOpType
AX = mybir.AxisListType
ENG = mybir.EngineType

P = 128
LAYERS = 2
T = 512
D = 1024
DK = D // P
FFN = 2816
FK = FFN // P
UNITS = FK // 2
EPS = 1e-6
HD = 64
CHUNK = 64
NCH = T // CHUNK
QT = 4
TAPS = 31
SC_TAPS = 3
WINDOWS = (2, 4, 8, 16)
UPAD = 16
MODS = 9

C_FFN1 = 0
C_FFN1_OUT = C_FFN1 + 2 * FK
C_PROJ = C_FFN1_OUT + FK
PROJ_TILES = 30
C_POOL = C_PROJ + PROJ_TILES
C_SC = C_POOL + 10
C_CONV = C_SC + 16
C_ATTN = C_CONV + 16
C_WO = C_ATTN + 16
C_FFN2 = C_WO + DK
C_FFN2_OUT = C_FFN2 + 2 * FK
CHUNKS = C_FFN2_OUT + FK
SLOTS = 4
assert CHUNKS % SLOTS == 0 and C_PROJ % SLOTS == 2 and C_SC % SLOTS == 2

ADA_FIRST = 2
ADA_STEP = 9
ADA_GROUPS = ADA_FIRST + LAYERS * ADA_STEP
HALVES = 2 * ADA_STEP
PIECES = 4

PAR = {}
_at = 0
for _name, _n in (("gain", 3 * DK), ("b_gate", 4 * DK), ("pool_scale", DK), ("conv_w", 4 * TAPS), ("conv_b", 4),
                  ("ln_g", 4), ("ln_b", 4), ("sc_w", 4 * SC_TAPS), ("q_gain", 1), ("k_gain", 1), ("sink", QT)):
    PAR[_name] = _at
    _at += _n
NPAR = _at
G_ADA_B = 0
G_C = ADA_GROUPS * DK
G_FREQ = G_C + DK
G_COUNT = G_FREQ + 1
NGLOBAL = G_COUNT + len(WINDOWS) * UPAD

TWO_PI = 6.283185307179586
TURN_MID = 2029 / 2 ** 20
TURN = (6.28125, TURN_MID, TWO_PI - 6.28125 - TURN_MID)
ROUND = 12582912.0

J_K, J_Q, J_V, J_U = 20, 21, 25, 26

USES = (
    ("ffn0", UNITS, (0, 1, 2, 3)),
    ("out0", 0, range(8)),
    ("proj", PROJ_TILES // 4, (0, 1, 2, 3)),
    ("proj_tail", 1, (0, 1)),
    ("norm0", 1, (4,)), ("norm1", 1, (5,)), ("norm2", 1, (4,)),
    ("norm3", 1, (5,)), ("rope0", 1, (6,)), ("norm4", 1, (4,)), ("rope1", 1, (7,)),
    ("rope2", 1, (6,)), ("v_turn", 1, (4, 5)), ("rope3", 1, (7,)), ("rope4", 1, (6,)),
    ("pool0", 1, range(8)),
    ("pool1", 1, range(8)),
    ("sc", 4, range(8)),
    ("pv", 1, (4, 5, 6, 7)),
    ("conv", 4, (0, 1, 2, 3)),
    ("attn", 4, (0, 1, 2, 3)),
    ("out1", 0, range(8)),
    ("ffn1", UNITS, (0, 1, 2, 3)),
    ("out2", 0, range(8)),
)
FIRST_USE, USES_OF = {}, [0] * 8
for _name, _times, _banks in USES:
    for _b in _banks:
        FIRST_USE[_name, _b] = USES_OF[_b]
        USES_OF[_b] += _times
NORM_BANK, ROPE_BANK = (4, 5, 4, 5, 4), (6, 7, 6, 7, 6)

def tiles_of(c):
    if C_POOL <= c < C_SC:
        return 4 if (c - C_POOL) % 5 == 0 else 8
    return 4 if C_SC <= c < C_WO and (c - C_SC) % 2 else 8


N_HALF = sum(tiles_of(c) == 4 for c in range(CHUNKS))
N_FULL = CHUNKS - N_HALF


class Signal:

    def __init__(self, nc, ctx, name, per_layer=0, start=0):
        self.sem = ctx.enter_context(nc.semaphore(name))
        self.per_layer, self.start = per_layer, start

    def __call__(self, l, n):
        return l * self.per_layer + (n + self.start)


class Bank(Signal):

    def __init__(self, nc, ctx, b):
        super().__init__(nc, ctx, f"bank_free{b}", USES_OF[b], 1)
        self.b = b

    def before(self, l, phase, time=0):
        return self(l, time + FIRST_USE[phase, self.b])

    def after(self, l, phase, time=0):
        return self(l, time + (FIRST_USE[phase, self.b] + 1))


def trunk_program(nc, io):
    ctx = ExitStack()
    with ctx:
        place = [(nc.sbuf_base + 31) // 32 * 32]

        def sb(name, shape, dt=F32):
            at = place[0]
            place[0] += (4 * int(np.prod(shape[1:])) + 31) // 32 * 32
            return nc.alloc_sbuf_tensor_at(name, shape, dt, offset=at)

        raw = [sb(f"weights_raw{s}", [P, 8, P]) for s in range(SLOTS)]
        whi = [sb(f"weights_hi{s}", [P, 8, P], F32R) for s in range(SLOTS)]
        wlo = [sb(f"weights_lo{s}", [P, 8, P], F32R) for s in range(SLOTS)]
        x = sb("x", [P, DK, T])
        h_hi = sb("h_hi", [P, DK, T], F32R)
        h_lo = sb("h_lo", [P, DK, T], F32R)
        tmp = [sb(f"tmp{i}", [P, T]) for i in range(4)]
        mats = sb("mats", [P, 4, P])
        ones, head_ones, half_turn, ident = (mats[:, i, :] for i in range(4))
        glob = sb("glob", [P, NGLOBAL])
        par = sb("par", [P, NPAR])
        mods = sb("mods", [P, ADA_GROUPS * DK])
        cond = sb("cond", [P, DK])
        eps = sb("eps", [P, 1])
        mod_gain = sb("mod_gain", [P, DK])
        mod_shift = sb("mod_shift", [P, DK])
        mod_gate = sb("mod_gate", [P, DK])
        neg_sink = sb("neg_sink", [P, QT])
        soft = sb("soft", [P, 5, NCH])

        region, REGION_KB = place[0], 98

        def at(name, kb, shape, dt=F32):
            assert kb * 1024 + 4 * np.prod(shape[1:]) <= REGION_KB * 1024
            return nc.alloc_sbuf_tensor_at(name, shape, dt, offset=region + int(kb * 1024))

        act_hi = at("act_hi", 0, [P, FK * T], F32R)
        act_lo = at("act_lo", 44, [P, FK * T], F32R)
        ada_buf = [at(f"ada_buf{b}", 88 + 4 * b, [P, 2, T]) for b in range(2)]
        ada_acc = at("ada_acc", 96, [P, T])
        ada_now = [at(f"ada_now{g}", 32 * g, [P, DK, D]) for g in range(ADA_FIRST)]
        angle = [at(f"angle{i}", 64 + 2 * i, [P, T]) for i in range(4)]
        angle_i = at("angle_i", 72, [P, T], I32)
        sc_hi, sc_lo = at("sc_hi", 0, [P, 4, T], F32R), at("sc_lo", 8, [P, 4, T], F32R)
        u_pad = [at(f"u_pad{g}", 16 + 2.125 * g, [P, UPAD + T]) for g in range(4)]
        window = [at(f"window{i}", 24.5 + 2.125 * i, [P, UPAD + T]) for i in range(2)]
        z_pad = [at(f"z_pad{i}", 32 + 2.125 * i, [P, TAPS - 1 + T]) for i in range(2)]
        s_pad = at("s_pad", 36.5, [P, SC_TAPS - 1 + T])
        s_conv = at("s_conv", 38.75, [P, T])
        sc_out = at("sc_out", 40.75, [P, T])
        odd_taps = at("odd_taps", 42.75, [P, T])
        pool_hi, pool_lo = at("pool_hi", 48, [P, 4, T], F32R), at("pool_lo", 56, [P, 4, T], F32R)
        q = at("q", 64, [P, QT * T])
        k_pad = at("k_pad", 72, [P, CHUNK + T])
        v_pad = at("v_pad", 74.25, [P, CHUNK + T])
        v_tok = at("v_tok", 76.5, [P, NCH, P])
        rope_tab = at("rope_tab", 80.5, [P, 2, T])
        conv_out = [at(f"conv_out{i}", 88.5 + 2 * i, [P, T]) for i in range(4)]
        pair = [at("pair0", 42.75, [P, T]), at("pair1", 86.5, [P, T])]
        conv_hi, conv_lo = at("conv_hi", 16, [P, 4, T], F32R), at("conv_lo", 24, [P, 4, T], F32R)
        merged = at("merged", 32, [P, DK * T])
        xc_sq = [at(f"xc_sq{i}", 80.5 + 2 * i, [P, T]) for i in range(2)]
        probs = at("probs", 84.5, [P, NCH, P])
        probs_t = at("probs_t", 48, [P, NCH, 2, QT, CHUNK])
        o_hi, o_lo = at("o_hi", 48, [P, QT, T], F32R), at("o_lo", 56, [P, QT, T], F32R)
        mixed_hi, mixed_lo = at("mixed_hi", 0, [P, DK * T], F32R), at("mixed_lo", 16, [P, DK * T], F32R)
        q_now = tmp[3]

        ps = [ctx.enter_context(nc.psum_tensor(f"bank{b}", [P, T], F32)) for b in range(8)]

        def sig(name, per_layer=0, start=0):
            return Signal(nc, ctx, name, per_layer, start)

        loaded = [sig(f"loaded{s}", 16 * (CHUNKS // SLOTS)) for s in range(SLOTS)]
        hi_done = sig("hi_done", CHUNKS)
        split = sig("split", CHUNKS, SLOTS)
        used = sig("used", CHUNKS, SLOTS)
        bank = [Bank(nc, ctx, b) for b in range(8)]
        x_loaded = sig("x_loaded")
        glob_loaded = sig("glob_loaded")
        ada_first_loaded = sig("ada_first_loaded")
        par_loaded = sig("par_loaded", 16)
        rope_loaded = sig("rope_loaded", 16)
        ada_loaded = [sig(f"ada_loaded{b}", 16 * (HALVES * PIECES // 2)) for b in range(2)]
        ada_free = sig("ada_free", HALVES * PIECES, 2)
        rope_stored = sig("rope_stored")
        out_stored = sig("out_stored")
        setup_step = sig("setup_step")
        angles_ready = sig("angles_ready")
        angle_sin = sig("angle_sin")
        cond_ready = sig("cond_ready")
        ada_first_ready = sig("ada_first_ready")
        ada_step = sig("ada_step", HALVES * PIECES)
        ada_sum = sig("ada_sum", HALVES)
        mods_done = sig("mods_done", HALVES, 1)
        coef_ready = sig("coef_ready", 3)
        gate_coef = sig("gate_coef", 3)
        square_ready = sig("square_ready", 3 * DK, DK)
        square_summed = sig("square_summed", 3 * DK, DK)
        norm_sum = sig("norm_sum", 3)
        rms_ready = sig("rms_ready", 3)
        inv_rms = sig("inv_rms", 3)
        xn_ready = sig("xn_ready", 3 * DK)
        h_hi_ready = sig("h_hi_ready", 3 * DK)
        h_ready = sig("h_ready", 3 * DK)
        act_hi_ready = sig("act_hi_ready", 2 * FK)
        act_ready = sig("act_ready", 2 * FK)
        out_tile = sig("out_tile", 3 * 6)
        x_updated = sig("x_updated", 3 * DK)
        pads_ready = sig("pads_ready", 1)
        conv_tap = sig("conv_tap", 4 * (TAPS + 1))
        sc_tap = sig("sc_tap", 4 * SC_TAPS)
        sc_out_ready = sig("sc_out_ready", 4)
        sc_hi_ready = sig("sc_hi_ready", 4)
        sc_ready = sig("sc_ready", 4)
        qk_square = sig("qk_square", 5)
        qk_norm = sig("qk_norm", 5)
        qk_inv = sig("qk_inv", 5)
        qk_normed = sig("qk_normed", 5)
        qk_turned = sig("qk_turned", 5)
        rope_part = sig("rope_part", 5)
        qk_ready = sig("qk_ready", 5)
        k_first = sig("k_first", 1)
        v_turned = sig("v_turned", 1)
        window_step = sig("window_step", 14)
        pool_out = sig("pool_out", 4)
        pool_hi_ready = sig("pool_hi_ready", 4)
        pool_ready = sig("pool_ready", 4)
        ln_sum = sig("ln_sum", 3)
        ln_mean = sig("ln_mean", 1)
        xc_ready = sig("xc_ready", 4)
        xc_square = sig("xc_square", 4)
        xc_summed = sig("xc_summed", 4)
        ln_var = sig("ln_var", 1)
        ln_rms = sig("ln_rms", 1)
        ln_inv = sig("ln_inv", 1)
        ln_y = sig("ln_y", 4)
        conv_silu = sig("conv_silu", 4)
        conv_ready = sig("conv_ready", 4)
        merged_ready = sig("merged_ready", 3 * DK, 1)
        q_now_ready = sig("q_now_ready", QT)
        scores_ready = sig("scores_ready", QT)
        max_found = sig("max_found", QT)
        neg_max = sig("neg_max", QT)
        exp_ready = sig("exp_ready", QT)
        total_ready = sig("total_ready", 2 * QT)
        probs_ready = sig("probs_ready", QT)
        probs_turned = sig("probs_turned", QT)
        pv_ready = sig("pv_ready", 1)
        waits_carried = sig("waits_carried")
        o_hi_ready = sig("o_hi_ready", 4)
        mixed_hi_ready = sig("mixed_hi_ready", DK)
        mixed_ready = sig("mixed_ready", DK)

        def loop(engine, first, last):
            return nc.Fori(first, last, engines=(engine,), hint_back_edge=True)

        def tile(flat, i):
            return flat[:, bass.ds(i * T, T)]

        def mod_cols(l, which):
            return mods[:, bass.ds(l * (MODS * DK) + which * DK, DK)]

        def par_col(name, i=0):
            return par[:, bass.ds(i + PAR[name], 1)]

        block = ctx.enter_context(nc.Block())

        @block.sync
        def _(sp):
            sp.dma_start(glob[:], io["glob"]).then_inc(glob_loaded.sem, 16)
            sp.dma_start(angle_i[:], io["positions"]).then_inc(glob_loaded.sem, 16)
            for g in range(ADA_FIRST):
                for half in range(2):
                    ks = slice(4 * half, 4 * half + 4)
                    sp.dma_start(ada_now[g][:, ks, :], io["ada_first"][g, :, ks, :]).then_inc(ada_first_loaded.sem, 16)
            sp.dma_start(mats[:], io["mats"]).then_inc(x_loaded.sem, 16)
            sp.dma_start(x[:], io["x"]).then_inc(x_loaded.sem, 16)

            def load(l, c, slot, full=None, half=None):
                sp.wait_ge(split.sem, split(l, c + (1 - SLOTS)))
                if half is None:
                    sp.dma_start(raw[slot][:], io["full"][l * N_FULL + full]).then_inc(loaded[slot].sem, 16)
                else:
                    sp.dma_start(raw[slot][:, 0:4, :], io["half"][l * N_HALF + half]).then_inc(loaded[slot].sem, 16)

            with loop(ENG.SP, 0, LAYERS) as l:
                for c in range(SLOTS):
                    load(l, c, c, c)
                sp.dma_start(par[:], io["par"][l]).then_inc(par_loaded.sem, 16)
                with loop(ENG.SP, 0, ADA_STEP) as u:
                    for j in range(SLOTS):
                        load(l, u * 4 + (SLOTS + j), j, u * 4 + (SLOTS + j))
                        for b in range(2):
                            piece = u * 8 + (2 * j + b)
                            sp.wait_ge(ada_free.sem, ada_free(l, piece - 1))
                            sp.dma_start(ada_buf[b][:], io["ada_rest"][l * (HALVES * PIECES) + piece]
                                         ).then_inc(ada_loaded[b].sem, 16)
                with loop(ENG.SP, ADA_STEP + 1, 20) as u:
                    for j in range(SLOTS):
                        load(l, u * 4 + j, j, u * 4 + j)
                sp.wait_ge(h_ready.sem, h_ready(l, DK + 1))
                sp.wait_ge(rope_stored.sem, 32)
                sp.dma_start(rope_tab[:], io["rope_scratch"]).then_inc(rope_loaded.sem, 16)
                with loop(ENG.SP, 20, C_POOL // SLOTS) as u:
                    for j in range(SLOTS):
                        load(l, u * 4 + j, j, u * 4 + j)
                full, half = C_POOL, 0
                for c in range(C_POOL, C_SC):
                    if tiles_of(c) == 4:
                        load(l, c, c % SLOTS, half=half)
                        half += 1
                    else:
                        load(l, c, c % SLOTS, full)
                        full += 1
                with loop(ENG.SP, 0, (C_WO - C_SC) // SLOTS) as u:
                    for j in range(SLOTS):
                        if j % 2:
                            load(l, u * 4 + (C_SC + j), (C_SC + j) % SLOTS, half=u * 2 + (half + j // 2))
                        else:
                            load(l, u * 4 + (C_SC + j), (C_SC + j) % SLOTS, u * 2 + (full + j // 2))
                full += (C_WO - C_SC) // 2
                rest = CHUNKS - C_WO
                with loop(ENG.SP, 0, rest // SLOTS) as u:
                    for j in range(SLOTS):
                        load(l, u * 4 + (C_WO + j), (C_WO + j) % SLOTS, u * 4 + (full + j))
                for j in range(rest // SLOTS * SLOTS, rest):
                    load(l, C_WO + j, (C_WO + j) % SLOTS, full + j)
            for m in range(DK):
                sp.wait_ge(x_updated.sem, x_updated(LAYERS - 1, 2 * DK + m + 1))
                sp.dma_start(io["out"][:, m, :], x[:, m, :]).then_inc(out_stored.sem, 16)
            sp.wait_ge(out_stored.sem, 16 * DK)

        @block.gpsimd
        def _(pool):
            pool.sem_inc(split.sem, SLOTS)

            def lo(l, c, slot, tiles=8):
                pool.wait_ge(hi_done.sem, hi_done(l, c + 1))
                nc.gpsimd.tensor_tensor(wlo[slot][:, 0:tiles, :], raw[slot][:, 0:tiles, :],
                                        whi[slot][:, 0:tiles, :].bitcast(F32), ALU.subtract).then_inc(split.sem, 1)

            with loop(ENG.Pool, 0, LAYERS) as l:
                with loop(ENG.Pool, 0, C_POOL // SLOTS) as u:
                    for j in range(SLOTS):
                        lo(l, u * 4 + j, j)
                for c in range(C_POOL, C_SC):
                    lo(l, c, c % SLOTS, tiles_of(c))
                with loop(ENG.Pool, 0, (C_WO - C_SC) // SLOTS) as u:
                    for j in range(SLOTS):
                        lo(l, u * 4 + (C_SC + j), (C_SC + j) % SLOTS, tiles_of(C_SC + j))
                rest = CHUNKS - C_WO
                with loop(ENG.Pool, 0, rest // SLOTS) as u:
                    for j in range(SLOTS):
                        lo(l, u * 4 + (C_WO + j), (C_WO + j) % SLOTS)
                for j in range(rest // SLOTS * SLOTS, rest):
                    lo(l, C_WO + j, (C_WO + j) % SLOTS)

        @block.scalar
        def _(act):
            def hi(l, c, slot, tiles=8):
                act.wait_ge(loaded[slot].sem, loaded[slot](l, (c - slot) * 4 + 16))
                act.wait_ge(used.sem, used(l, c + (1 - SLOTS)))
                nc.scalar.activation(whi[slot][:, 0:tiles, :], raw[slot][:, 0:tiles, :],
                                     ACT.Copy).then_inc(hi_done.sem, 1)

            def norm(l, s):
                act.wait_ge(norm_sum.sem, norm_sum(l, s + 1))
                nc.scalar.activation(ps[5][:], ps[4][:], ACT.Sqrt, bias=eps[:, 0:1],
                                     scale=1.0 / D).then_inc(rms_ready.sem, 1)
                act.wait_ge(coef_ready.sem, coef_ready(l, s + 1))
                for k in range(DK):
                    n = s * DK + k
                    act.wait_ge(xn_ready.sem, xn_ready(l, n + 1))
                    if k >= 2:
                        act.wait_ge(h_ready.sem, h_ready(l, n - 1))
                    nc.scalar.activation(tmp[2 + k % 2][:], tmp[k % 2][:], ACT.Identity,
                                         bias=mod_shift[:, k:k + 1], scale=mod_gain[:, k:k + 1])
                    nc.scalar.activation(h_hi[:, k, :], tmp[k % 2][:], ACT.Identity, bias=mod_shift[:, k:k + 1],
                                         scale=mod_gain[:, k:k + 1]).then_inc(h_hi_ready.sem, 1)

            def ffn(l, f, c0):
                with loop(ENG.Activation, 0, UNITS) as u:
                    for p in range(2):
                        c = c0 + 2 * p
                        hi(l, u * 4 + (c + 4), c % SLOTS)
                        nc.scalar.activation(tmp[p][:], ps[2 * p][:], ACT.Silu).then_inc(bank[2 * p].sem, 1)
                        hi(l, u * 4 + (c + 5), (c + 1) % SLOTS)
                        act.wait_ge(bank[2 * p + 1].sem, bank[2 * p + 1].after(l, f"ffn{f}", u))
                        nc.scalar.activation(tile(act_hi, u * 2 + p), tmp[2 + p][:],
                                             ACT.Copy).then_inc(act_hi_ready.sem, 1)

            def out_product(l, s, c0, n, last=False):
                for half in range(2):
                    c = c0 + half * n
                    ahead = n - (SLOTS if last and half == 1 else 0)
                    loops = ahead // SLOTS if ahead >= 2 * SLOTS else 0
                    if loops:
                        with loop(ENG.Activation, 0, loops) as u:
                            for j in range(SLOTS):
                                hi(l, u * 4 + (c + 4 + j), (c + j) % SLOTS)
                    for j in range(loops * SLOTS, ahead):
                        hi(l, c + 4 + j, (c + j) % SLOTS)
                    for m in range(4 * half, 4 * half + 4):
                        act.wait_ge(x_updated.sem, x_updated(l, s * DK + m + 1))
                        act.wait_ge(square_summed.sem, square_summed(l, s * DK + m - 1))
                        nc.scalar.activation(tmp[m % 2][:], x[:, m, :], ACT.Square).then_inc(square_ready.sem, 1)

            act.wait_ge(glob_loaded.sem, 32)
            nc.scalar.activation(cond[:], glob[:, G_C:G_C + DK], ACT.Silu).then_inc(cond_ready.sem, 1)
            act.wait_ge(angles_ready.sem, 2)
            for i in range(2):
                nc.scalar.activation(angle[2 + i][:], angle[i][:], ACT.Sin).then_inc(angle_sin.sem, 1)
            for i in range(2):
                act.wait_ge(angle_sin.sem, i + 1)
                act.dma_start(io["rope_scratch"][:, i, :], angle[2 + i][:]).then_inc(rope_stored.sem, 16)
            act.wait_ge(x_loaded.sem, 32)
            for m in range(DK):
                if m >= 2:
                    act.wait_ge(square_summed.sem, m - 1)
                nc.scalar.activation(tmp[m % 2][:], x[:, m, :], ACT.Square).then_inc(square_ready.sem, 1)

            with loop(ENG.Activation, 0, LAYERS) as l:
                for c in range(SLOTS):
                    hi(l, c, c)
                norm(l, 0)
                ffn(l, 0, C_FFN1)
                out_product(l, 0, C_FFN1_OUT, UNITS)
                norm(l, 1)

                def step(j):
                    c = C_PROJ + j + SLOTS
                    hi(l, c, c % SLOTS, tiles_of(c))

                def sc_high(i):
                    act.wait_ge(sc_out_ready.sem, sc_out_ready(l, i + 1))
                    nc.scalar.activation(sc_hi[:, i, :], sc_out[:], ACT.Copy).then_inc(sc_hi_ready.sem, 1)

                for i in range(4):
                    j = 5 * i
                    step(j)
                    step(j + 1)
                    b = (j + 1) % 4
                    nc.scalar.activation(tmp[0][:], ps[b][:], ACT.Sigmoid).then_inc(bank[b].sem, 1)
                    step(j + 2)
                    b = (j + 2) % 4
                    nc.scalar.activation(tmp[1][:], ps[b][:], ACT.Copy).then_inc(bank[b].sem, 1)
                    step(j + 3)
                    if i >= 1:
                        sc_high(i - 1)
                    step(j + 4)
                    b = (j + 4) % 4
                    nc.scalar.activation(tmp[2][:], ps[b][:], ACT.Copy).then_inc(bank[b].sem, 1)

                def qk_root(n):
                    b = NORM_BANK[n]
                    act.wait_ge(qk_norm.sem, qk_norm(l, n + 1))
                    if n >= 1:
                        act.wait_ge(qk_inv.sem, qk_inv(l, n))
                    nc.scalar.activation(tmp[2][:], ps[b][:], ACT.Sqrt, bias=eps[:, 0:1],
                                         scale=1.0 / HD).then_inc(bank[b].sem, 1)

                for j in range(J_K, PROJ_TILES):
                    step(j)
                    n, b = j - J_K, j % 4
                    if n < 5:
                        if n == 1:
                            sc_high(3)
                        if n >= 2:
                            act.wait_ge(qk_norm.sem, qk_norm(l, n - 1))
                        nc.scalar.activation(tmp[n % 2][:], ps[b][:], ACT.Square).then_inc(qk_square.sem, 1)
                        dst = k_pad[:, CHUNK:] if n == 0 else tile(q, n - 1)
                    elif j == J_V:
                        dst = v_pad[:, CHUNK:]
                    else:
                        dst = u_pad[j - J_U][:, UPAD:]
                    nc.scalar.activation(dst, ps[b][:], ACT.Copy).then_inc(bank[b].sem, 1)
                    if 2 <= n < 7:
                        qk_root(n - 2)
                act.wait_ge(v_turned.sem, v_turned(l, 1))
                for b in range(2):
                    nc.scalar.activation(v_tok[:, 4 * b:4 * b + 4, :], ps[4 + b][:].rearrange(
                        "p (c d) -> p c d", c=4), ACT.Copy).then_inc(bank[4 + b].sem, 1)
                for g in range(4):
                    act.wait_ge(pool_out.sem, pool_out(l, g + 1))
                    nc.scalar.activation(pool_hi[:, g, :], pair[g % 2][:], ACT.Copy).then_inc(pool_hi_ready.sem, 1)

                def pool_branch(half):
                    c = C_POOL + 5 * half
                    hi(l, c + 4, c % SLOTS, tiles_of(c + 4))
                    for i in range(4):
                        m = 4 * half + i
                        hi(l, c + 5 + i, (c + 1 + i) % SLOTS, tiles_of(c + 5 + i))
                        if m >= 2:
                            before = 4 + (m - 2) % 4
                            act.wait_ge(bank[before].sem, bank[before].after(l, f"pool{(m - 2) // 4}"))
                        nc.scalar.activation(tmp[m % 2][:], ps[i][:], ACT.Sigmoid,
                                             bias=par_col("b_gate", DK + m)).then_inc(bank[i].sem, 1)

                pool_branch(0)
                for i in range(4):
                    act.wait_ge(xc_ready.sem, xc_ready(l, i + 1))
                    if i >= 2:
                        act.wait_ge(xc_summed.sem, xc_summed(l, i - 1))
                    nc.scalar.activation(xc_sq[i % 2][:], conv_out[i][:], ACT.Square).then_inc(xc_square.sem, 1)
                pool_branch(1)
                act.wait_ge(ln_var.sem, ln_var(l, 1))
                nc.scalar.activation(xc_sq[0][:], ps[3][:], ACT.Sqrt, bias=eps[:, 0:1],
                                     scale=1.0 / (4 * P)).then_inc(ln_rms.sem, 1)
                for i in range(4):
                    act.wait_ge(ln_y.sem, ln_y(l, i + 1))
                    nc.scalar.activation(conv_hi[:, i, :], conv_out[i][:], ACT.Silu, bias=par_col("ln_b", i),
                                         scale=par_col("ln_g", i))
                    nc.scalar.activation(conv_out[i][:], conv_out[i][:], ACT.Silu, bias=par_col("ln_b", i),
                                         scale=par_col("ln_g", i)).then_inc(conv_silu.sem, 1)
                act.wait_ge(bank[7].sem, bank[7].after(l, "pool1"))

                def pair_step(l, p, name, c0, which, scores=False, split_merged=False, last=False):
                    if scores:
                        nc.scalar.activation(q_now[:], tile(q, p), ACT.Copy).then_inc(q_now_ready.sem, 1)
                    for e in range(2):
                        c = c0 + 2 * e
                        hi(l, p * 4 + (c + 4), c % SLOTS)
                        act.wait_ge(bank[2 * e + 1].sem, bank[2 * e + 1].before(l, name, p))
                        nc.scalar.activation(tmp[e][:], ps[2 * e][:], ACT.Sigmoid,
                                             bias=par_col("b_gate", p * 2 + (which * DK + e))
                                             ).then_inc(bank[2 * e].sem, 1)
                        hi(l, p * 4 + (c + 5), (c + 1) % SLOTS, 8 if last else 4)
                        if scores and e == 0:
                            act.wait_ge(neg_max.sem, neg_max(l, p + 1))
                            for ch in range(NCH):
                                b = 4 + ch // 4
                                first = CHUNK if ch == 0 else 0
                                ins = nc.scalar.activation(
                                    probs[:, ch, first:], ps[b][:, (ch % 4) * P + first:(ch % 4 + 1) * P], ACT.Exp,
                                    bias=soft[:, 1, ch:ch + 1], scale=HD ** -0.5, accum_out=soft[:, 2, ch:ch + 1])
                                if ch % 4 == 3:
                                    ins.then_inc(bank[b].sem, 1)
                            nc.scalar.activation(soft[:, 3, :], soft[:, 1, :], ACT.Exp,
                                                 bias=par_col("sink", p)).then_inc(exp_ready.sem, 1)
                        if split_merged:
                            act.wait_ge(merged_ready.sem, merged_ready(l, p * 2 + (2 * DK + e + 1)))
                            nc.scalar.activation(tile(mixed_hi, p * 2 + e), tile(merged, p * 2 + e),
                                                 ACT.Copy).then_inc(mixed_hi_ready.sem, 1)
                    if scores:
                        act.wait_ge(probs_turned.sem, probs_turned(l, p + 1))
                        for b in range(2):
                            nc.scalar.activation(probs_t[:, 4 * b:4 * b + 4, :, bass.ds(p, 1), :],
                                                 ps[6 + b][:].rearrange("p (c g t) -> p c g t", c=4, g=2),
                                                 ACT.Copy).then_inc(bank[6 + b].sem, 1)

                with loop(ENG.Activation, 0, 4) as p:
                    pair_step(l, p, "sc", C_SC, 3, scores=True)
                act.wait_ge(pv_ready.sem, pv_ready(l, 1))
                for b in range(4):
                    nc.scalar.activation(o_hi[:, :, P * b:P * b + P].rearrange("p i (c t) -> p c i t", c=2),
                                         ps[4 + b][:].rearrange("p (c i t) -> p c i t", c=2, i=QT),
                                         ACT.Copy).then_inc(o_hi_ready.sem, 1)
                with loop(ENG.Activation, 0, 4) as p:
                    pair_step(l, p, "conv", C_CONV, 2)
                with loop(ENG.Activation, 0, 3) as p:
                    pair_step(l, p, "attn", C_ATTN, 0, split_merged=True)
                pair_step(l, 3, "attn", C_ATTN, 0, split_merged=True, last=True)
                out_product(l, 1, C_WO, DK // 2)
                norm(l, 2)
                ffn(l, 1, C_FFN2)
                out_product(l, 2, C_FFN2_OUT, UNITS, last=True)

        @block.vector
        def _(dve):
            V = nc.vector
            links = [0]

            def link(ins):
                links[0] += 1
                ins.then_inc(setup_step.sem, 1)
                dve.wait_ge(setup_step.sem, links[0])

            dve.sem_inc(ada_free.sem, 2)
            dve.sem_inc(merged_ready.sem, 1)
            link(V.memset(eps[:], EPS))
            dve.wait_ge(glob_loaded.sem, 32)
            a, turns = angle[0], angle[1]
            link(V.tensor_copy(a[:], angle_i[:]))
            link(V.tensor_scalar(a[:], a[:], glob[:, G_FREQ:G_FREQ + 1], None, ALU.mult))
            for unit in (4096.0, 1.0):
                link(V.tensor_scalar(turns[:], a[:], 1.0 / (TWO_PI * unit), ROUND, ALU.mult, ALU.add))
                link(V.tensor_scalar(turns[:], turns[:], ROUND, None, ALU.subtract))
                for part in TURN:
                    link(V.scalar_tensor_tensor(a[:], turns[:], -part * unit, a[:], ALU.mult, ALU.add))
            V.tensor_scalar(angle[1][:], a[:], 3.1415925, -3.1415925, ALU.min, ALU.max).then_inc(angles_ready.sem, 1)
            dve.wait_ge(angles_ready.sem, 1)
            link(V.scalar_tensor_tensor(a[:], angle[1][:], -1.0, angle[1][:], ALU.mult, ALU.max))
            V.tensor_scalar(a[:], a[:], -1.0, TWO_PI / 4, ALU.mult, ALU.add).then_inc(angles_ready.sem, 1)
            for m in range(DK):
                dve.wait_ge(square_ready.sem, m + 1)
                if m == 0:
                    V.tensor_copy(tmp[2][:], tmp[0][:]).then_inc(square_summed.sem, 1)
                else:
                    dve.wait_ge(square_summed.sem, m)
                    V.tensor_tensor(tmp[2][:], tmp[2][:], tmp[m % 2][:], ALU.add).then_inc(square_summed.sem, 1)
            dve.wait_ge(ada_first_ready.sem, 1)
            n = ADA_FIRST * DK
            V.tensor_tensor(mods[:, 0:n], ps[7][:, 0:n], glob[:, G_ADA_B:G_ADA_B + n],
                            ALU.add).then_inc(mods_done.sem, 1)
            dve.wait_ge(rope_stored.sem, 32)

            def norm(l, s):
                dve.wait_ge(mods_done.sem, mods_done(l, HALVES if s else 0))
                dve.wait_ge(par_loaded.sem, par_loaded(l, 16))
                V.scalar_tensor_tensor(mod_gain[:], mod_cols(l, 3 * s + 1), 1.0,
                                       par[:, PAR["gain"] + s * DK:PAR["gain"] + s * DK + DK], ALU.add, ALU.mult)
                V.tensor_copy(mod_shift[:], mod_cols(l, 3 * s)).then_inc(coef_ready.sem, 1)
                dve.wait_ge(rms_ready.sem, rms_ready(l, s + 1))
                V.reciprocal(ps[5][:], ps[5][:]).then_inc(inv_rms.sem, 1)
                dve.wait_ge(inv_rms.sem, inv_rms(l, s + 1))
                for k in range(DK + 1):
                    n = s * DK + k
                    if k < DK:
                        if k >= 2:
                            dve.wait_ge(h_hi_ready.sem, h_hi_ready(l, n - 1))
                        V.tensor_tensor(tmp[k % 2][:], x[:, k, :], ps[5][:], ALU.mult).then_inc(xn_ready.sem, 1)
                    if k >= 1:
                        dve.wait_ge(h_hi_ready.sem, h_hi_ready(l, n))
                        V.tensor_tensor(h_lo[:, k - 1, :], tmp[2 + (k - 1) % 2][:],
                                        h_hi[:, k - 1, :].bitcast(F32), ALU.subtract).then_inc(h_ready.sem, 1)

            def ffn(l, f, c0):
                def product(u, p):
                    dve.wait_ge(used.sem, used(l, u * 4 + (c0 + 2 * p + 2)))
                    dve.wait_ge(bank[2 * p].sem, bank[2 * p].after(l, f"ffn{f}", u))
                    V.tensor_tensor(tmp[2 + p][:], tmp[p][:], ps[2 * p + 1][:],
                                    ALU.mult).then_inc(bank[2 * p + 1].sem, 1)

                def low(u, p):
                    n = u * 2 + p
                    dve.wait_ge(act_hi_ready.sem, act_hi_ready(l, n + (f * FK + 1)))
                    V.tensor_tensor(tile(act_lo, n), tmp[2 + p][:], tile(act_hi, n).bitcast(F32),
                                    ALU.subtract).then_inc(act_ready.sem, 1)

                def store_mods(h):
                    dve.wait_ge(ada_sum.sem, ada_sum(l, h + 1))
                    col = l * (HALVES * 4) + (h * 4 + ADA_FIRST * DK)
                    V.tensor_tensor(mods[:, bass.ds(col, 4)], ps[7][:, 0:4], glob[:, bass.ds(col, 4)],
                                    ALU.add).then_inc(mods_done.sem, 1)

                def ada(h):
                    for i in range(PIECES):
                        piece = h * PIECES + i
                        b = i % 2
                        dve.wait_ge(ada_loaded[b].sem, ada_loaded[b](l, h * (16 * PIECES // 2) + 16 * (i // 2 + 1)))
                        if i == 0:
                            V.tensor_scalar(ada_acc[:], ada_buf[b][:, 0, :], cond[:, 0:1], None,
                                            ALU.mult).then_inc(ada_step.sem, 1)
                        else:
                            dve.wait_ge(ada_free.sem, ada_free(l, piece))
                            V.scalar_tensor_tensor(ada_acc[:], ada_buf[b][:, 0, :], cond[:, 2 * i:2 * i + 1],
                                                   ada_acc[:], ALU.mult, ALU.add).then_inc(ada_step.sem, 1)
                        dve.wait_ge(ada_step.sem, ada_step(l, piece + 1))
                        V.scalar_tensor_tensor(ada_acc[:], ada_buf[b][:, 1, :], cond[:, 2 * i + 1:2 * i + 2],
                                               ada_acc[:], ALU.mult, ALU.add).then_inc(ada_free.sem, 1)

                def unit(u, store, more):
                    for p in range(2):
                        product(u, p)
                        if store[p]:
                            store_mods(u * 2 + (p - 1))
                        if more[p]:
                            ada(u * 2 + p)
                        low(u, p)

                if f == 0:
                    unit(0, (False, True), (True, True))
                    with loop(ENG.DVE, 1, ADA_STEP) as u:
                        unit(u, (True, True), (True, True))
                    unit(ADA_STEP, (True, False), (False, False))
                    unit(ADA_STEP + 1, (False, False), (False, False))
                else:
                    with loop(ENG.DVE, 0, UNITS) as u:
                        unit(u, (False, False), (False, False))

            def add_square(l, s, m):
                dve.wait_ge(square_ready.sem, square_ready(l, s * DK + m + 1))
                if m == 0:
                    V.tensor_copy(tmp[2][:], tmp[0][:]).then_inc(square_summed.sem, 1)
                else:
                    dve.wait_ge(square_summed.sem, square_summed(l, s * DK + m))
                    V.tensor_tensor(tmp[2][:], tmp[2][:], tmp[m % 2][:], ALU.add).then_inc(square_summed.sem, 1)

            def out_product(l, s, c0, n):
                V.tensor_scalar(mod_gate[:], mod_cols(l, 3 * s + 2), 1.0 if s == 1 else 0.5, None,
                                ALU.mult).then_inc(gate_coef.sem, 1)
                dve.wait_ge(gate_coef.sem, gate_coef(l, s + 1))
                for half in range(2):
                    for i in range(4):
                        m = 4 * half + i
                        if i < 3:
                            dve.wait_ge(out_tile.sem, out_tile(l, s * 6 + half * 3 + i + 1))
                        else:
                            dve.wait_ge(used.sem, used(l, c0 + (half + 1) * n))
                        V.scalar_tensor_tensor(x[:, m, :], ps[4 * (1 - half) + i][:], mod_gate[:, m:m + 1],
                                               x[:, m, :], ALU.mult, ALU.add).then_inc(x_updated.sem, 1)
                        if m >= 1:
                            add_square(l, s, m - 1)
                add_square(l, s, DK - 1)

            with loop(ENG.DVE, 0, LAYERS) as l:
                norm(l, 0)
                ffn(l, 0, C_FFN1)
                out_product(l, 0, C_FFN1_OUT, UNITS)
                norm(l, 1)

                for pad in [z[:, 0:TAPS - 1] for z in z_pad] + [s_pad[:, 0:SC_TAPS - 1], v_pad[:, 0:CHUNK]] \
                        + [probs[:, 0, 0:CHUNK]] + [u[:, 0:UPAD] for u in u_pad]:
                    V.memset(pad, 0.0)
                V.tensor_scalar(neg_sink[:], par[:, PAR["sink"]:PAR["sink"] + QT], -1.0, None,
                                ALU.mult).then_inc(pads_ready.sem, 1)
                dve.wait_ge(pads_ready.sem, pads_ready(l, 1))

                def proj_bank(j):
                    phase = ("proj", j // 4) if j < 28 else ("proj_tail", 0)
                    return j % 4, phase

                def read_by_scalar(j):
                    b, (phase, time) = proj_bank(j)
                    dve.wait_ge(bank[b].sem, bank[b].after(l, phase, time))

                def sc_low(i):
                    dve.wait_ge(sc_hi_ready.sem, sc_hi_ready(l, i + 1))
                    V.tensor_tensor(sc_lo[:, i, :], sc_out[:], sc_hi[:, i, :].bitcast(F32),
                                    ALU.subtract).then_inc(sc_ready.sem, 1)

                for i in range(4):
                    j = 5 * i
                    z, acc = z_pad[i % 2], (conv_out[i], odd_taps)
                    read_by_scalar(j + 1)
                    V.tensor_tensor(z[:, TAPS - 1:], ps[j % 4][:], tmp[0][:], ALU.mult).then_inc(bank[j % 4].sem, 1)
                    read_by_scalar(j)
                    for t in range(TAPS):
                        src, w = z[:, t:t + T], par_col("conv_w", i * TAPS + t)
                        if t >= 2:
                            dve.wait_ge(conv_tap.sem, conv_tap(l, i * (TAPS + 1) + t - 1))
                            ins = V.scalar_tensor_tensor(acc[t % 2][:], src, w, acc[t % 2][:], ALU.mult, ALU.add)
                        elif t == 1:
                            if i >= 1:
                                dve.wait_ge(conv_tap.sem, conv_tap(l, i * (TAPS + 1)))
                            ins = V.tensor_scalar(acc[1][:], src, w, None, ALU.mult)
                        else:
                            ins = V.tensor_scalar(acc[0][:], src, w, par_col("conv_b", i), ALU.mult, ALU.add)
                        ins.then_inc(conv_tap.sem, 1)
                    dve.wait_ge(conv_tap.sem, conv_tap(l, i * (TAPS + 1) + TAPS))
                    V.tensor_tensor(acc[0][:], acc[0][:], acc[1][:], ALU.add).then_inc(conv_tap.sem, 1)
                    if i >= 1:
                        sc_low(i - 1)
                    dve.wait_ge(used.sem, used(l, C_PROJ + j + 4))
                    read_by_scalar(j + 2)
                    b = (j + 3) % 4
                    V.tensor_tensor(s_pad[:, SC_TAPS - 1:], ps[b][:], tmp[1][:], ALU.mult).then_inc(bank[b].sem, 1)
                    read_by_scalar(j + 3)
                    for t in range(SC_TAPS):
                        src, w = s_pad[:, t:t + T], par_col("sc_w", i * SC_TAPS + t)
                        if t == 0:
                            if i >= 1:
                                dve.wait_ge(sc_out_ready.sem, sc_out_ready(l, i))
                            V.tensor_scalar(s_conv[:], src, w, None, ALU.mult).then_inc(sc_tap.sem, 1)
                        else:
                            V.scalar_tensor_tensor(s_conv[:], src, w, s_conv[:], ALU.mult,
                                                   ALU.add).then_inc(sc_tap.sem, 1)
                        dve.wait_ge(sc_tap.sem, sc_tap(l, i * SC_TAPS + t + 1))
                    read_by_scalar(j + 4)
                    if i >= 1:
                        dve.wait_ge(sc_ready.sem, sc_ready(l, i))
                    V.tensor_tensor(sc_out[:], s_conv[:], tmp[2][:], ALU.mult).then_inc(sc_out_ready.sem, 1)

                def rotate(n):
                    raw_qk = k_pad[:, CHUNK:] if n == 0 else tile(q, n - 1)
                    if n >= 1:
                        dve.wait_ge(qk_ready.sem, qk_ready(l, n))
                    V.tensor_tensor(pair[0][:], raw_qk, rope_tab[:, 0, :], ALU.mult).then_inc(rope_part.sem, 1)
                    dve.wait_ge(qk_turned.sem, qk_turned(l, n + 1))
                    b = ROPE_BANK[n]
                    V.tensor_tensor(pair[1][:], ps[b][:], rope_tab[:, 1, :], ALU.mult).then_inc(bank[b].sem, 1)
                    dve.wait_ge(rope_part.sem, rope_part(l, n + 1))
                    dve.wait_ge(bank[b].sem, bank[b].after(l, f"rope{n}"))
                    V.tensor_tensor(raw_qk, pair[0][:], pair[1][:], ALU.add).then_inc(qk_ready.sem, 1)

                for n in range(6):
                    if n < 5:
                        raw_qk = k_pad[:, CHUNK:] if n == 0 else tile(q, n - 1)
                        b = NORM_BANK[n]
                        dve.wait_ge(bank[b].sem, bank[b].after(l, f"norm{n}"))
                        if n >= 1:
                            dve.wait_ge(qk_normed.sem, qk_normed(l, n))
                        V.reciprocal(tmp[3][:], tmp[2][:]).then_inc(qk_inv.sem, 1)
                        dve.wait_ge(qk_inv.sem, qk_inv(l, n + 1))
                        V.scalar_tensor_tensor(raw_qk, raw_qk, par_col("q_gain" if n else "k_gain"), tmp[3][:],
                                               ALU.mult, ALU.mult).then_inc(qk_normed.sem, 1)
                    if n == 0:
                        sc_low(3)
                        dve.wait_ge(rope_loaded.sem, rope_loaded(l, 16))
                    else:
                        dve.wait_ge(qk_normed.sem, qk_normed(l, n))
                        rotate(n - 1)
                    if n == 1:
                        dve.wait_ge(qk_ready.sem, qk_ready(l, 1))
                        V.tensor_copy(k_pad[:, 0:CHUNK], k_pad[:, CHUNK:2 * CHUNK]).then_inc(k_first.sem, 1)

                def pool_low(g):
                    dve.wait_ge(pool_hi_ready.sem, pool_hi_ready(l, g + 1))
                    V.tensor_tensor(pool_lo[:, g, :], pair[g % 2][:], pool_hi[:, g, :].bitcast(F32),
                                    ALU.subtract).then_inc(pool_ready.sem, 1)

                steps = 0
                for g, w in enumerate(WINDOWS):
                    read_by_scalar(J_U + g)
                    if g >= 1:
                        dve.wait_ge(pool_out.sem, pool_out(l, g))
                    src, start = u_pad[g], 0
                    for st in range(g + 1):
                        start += 2 ** st
                        V.tensor_tensor(window[st % 2][:, start:], src[:, start:], src[:, start - 2 ** st:UPAD + T - 2 ** st],
                                        ALU.add).then_inc(window_step.sem, 1)
                        steps += 1
                        dve.wait_ge(window_step.sem, window_step(l, steps))
                        src = window[st % 2]
                    col = G_COUNT + g * UPAD
                    V.tensor_tensor(src[:, UPAD:2 * UPAD], src[:, UPAD:2 * UPAD], glob[:, col:col + UPAD],
                                    ALU.mult).then_inc(window_step.sem, 1)
                    steps += 1
                    dve.wait_ge(window_step.sem, window_step(l, steps))
                    if g >= 2:
                        dve.wait_ge(pool_ready.sem, pool_ready(l, g - 1))
                    else:
                        dve.wait_ge(qk_ready.sem, qk_ready(l, 5))
                    V.scalar_tensor_tensor(pair[g % 2][:], src[:, UPAD:], 1.0 / w, u_pad[g][:, UPAD:], ALU.mult,
                                           ALU.subtract).then_inc(pool_out.sem, 1)
                    if g >= 1:
                        pool_low(g - 1)
                pool_low(3)

                dve.wait_ge(pool_ready.sem, pool_ready(l, 4))
                for i in range(1, 4):
                    if i >= 2:
                        dve.wait_ge(ln_sum.sem, ln_sum(l, i - 1))
                    V.tensor_tensor(pair[1][:], conv_out[0][:] if i == 1 else pair[1][:], conv_out[i][:],
                                    ALU.add).then_inc(ln_sum.sem, 1)

                def pool_merge(half):
                    dve.wait_ge(used.sem, used(l, C_POOL + 5 * half + 1))
                    for i in range(4):
                        m = 4 * half + i
                        dve.wait_ge(bank[i].sem, bank[i].after(l, f"pool{half}"))
                        V.scalar_tensor_tensor(tile(merged, m), ps[4 + i][:], par_col("pool_scale", m),
                                               tmp[m % 2][:], ALU.mult, ALU.mult).then_inc(bank[4 + i].sem, 1)

                pool_merge(0)
                dve.wait_ge(ln_mean.sem, ln_mean(l, 1))
                for i in range(4):
                    V.scalar_tensor_tensor(conv_out[i][:], ps[3][:], -1.0 / (4 * P), conv_out[i][:], ALU.mult,
                                           ALU.add).then_inc(xc_ready.sem, 1)
                for i in range(4):
                    dve.wait_ge(xc_square.sem, xc_square(l, i + 1))
                    if i == 0:
                        V.tensor_copy(pair[1][:], xc_sq[0][:]).then_inc(xc_summed.sem, 1)
                    else:
                        dve.wait_ge(xc_summed.sem, xc_summed(l, i))
                        V.tensor_tensor(pair[1][:], pair[1][:], xc_sq[i % 2][:], ALU.add).then_inc(xc_summed.sem, 1)
                pool_merge(1)
                dve.wait_ge(ln_rms.sem, ln_rms(l, 1))
                V.reciprocal(xc_sq[1][:], xc_sq[0][:]).then_inc(ln_inv.sem, 1)
                dve.wait_ge(ln_inv.sem, ln_inv(l, 1))
                for i in range(4):
                    V.tensor_tensor(conv_out[i][:], conv_out[i][:], xc_sq[1][:], ALU.mult).then_inc(ln_y.sem, 1)
                for i in range(4):
                    dve.wait_ge(conv_silu.sem, conv_silu(l, i + 1))
                    V.tensor_tensor(conv_lo[:, i, :], conv_out[i][:], conv_hi[:, i, :].bitcast(F32),
                                    ALU.subtract).then_inc(conv_ready.sem, 1)

                def merge(p, e, name, c0, n0):
                    dve.wait_ge(used.sem, used(l, p * 4 + (c0 + 2 * e + 2)))
                    dve.wait_ge(bank[2 * e].sem, bank[2 * e].after(l, name, p))
                    y = bank[2 * e + 1]
                    dve.wait_ge(merged_ready.sem, merged_ready(l, p * 2 + (n0 + e)))
                    V.tensor_tensor(tmp[2][:], tmp[e][:], ps[2 * e + 1][:], ALU.mult).then_inc(y.sem, 1)
                    dve.wait_ge(y.sem, y.after(l, name, p))
                    V.tensor_tensor(tile(merged, p * 2 + e), tile(merged, p * 2 + e), tmp[2][:],
                                    ALU.add).then_inc(merged_ready.sem, 1)

                with loop(ENG.DVE, 0, 4) as p:
                    dve.wait_ge(scores_ready.sem, scores_ready(l, p + 1))
                    for b in range(2):
                        ins = V.tensor_reduce(soft[:, 0, 4 * b:4 * b + 4],
                                              ps[4 + b][:].rearrange("p (c k) -> p c k", c=4), AX.X, ALU.max)
                    ins.then_inc(max_found.sem, 1)
                    dve.wait_ge(max_found.sem, max_found(l, p + 1))
                    V.tensor_scalar(soft[:, 1, :], soft[:, 0, :], -(HD ** -0.5), neg_sink[:, bass.ds(p, 1)],
                                    ALU.mult, ALU.min).then_inc(neg_max.sem, 1)
                    merge(p, 0, "sc", C_SC, 0)
                    dve.wait_ge(exp_ready.sem, exp_ready(l, p + 1))
                    V.tensor_tensor(soft[:, 4, :], soft[:, 2, :], soft[:, 3, :], ALU.add).then_inc(total_ready.sem, 1)
                    dve.wait_ge(total_ready.sem, total_ready(l, p * 2 + 1))
                    V.reciprocal(soft[:, 4, :], soft[:, 4, :]).then_inc(total_ready.sem, 1)
                    dve.wait_ge(total_ready.sem, total_ready(l, p * 2 + 2))
                    V.tensor_tensor(probs[:], probs[:], soft[:, 4, :].unsqueeze(2).broadcast_to((P, NCH, P)),
                                    ALU.mult).then_inc(probs_ready.sem, 1)
                    merge(p, 1, "sc", C_SC, 0)
                for b in range(4):
                    dve.wait_ge(o_hi_ready.sem, o_hi_ready(l, b + 1))
                    tokens = slice(P * b, P * b + P)
                    V.tensor_tensor(o_lo[:, :, tokens].rearrange("p i (c t) -> p c i t", c=2),
                                    ps[4 + b][:].rearrange("p (c i t) -> p c i t", c=2, i=QT),
                                    o_hi[:, :, tokens].bitcast(F32).rearrange("p i (c t) -> p c i t", c=2),
                                    ALU.subtract).then_inc(bank[4 + b].sem, 1)
                with loop(ENG.DVE, 0, 4) as p:
                    for e in range(2):
                        merge(p, e, "conv", C_CONV, DK)
                with loop(ENG.DVE, 0, 4) as p:
                    for e in range(2):
                        merge(p, e, "attn", C_ATTN, 2 * DK)
                        dve.wait_ge(mixed_hi_ready.sem, mixed_hi_ready(l, p * 2 + (e + 1)))
                        V.tensor_tensor(tile(mixed_lo, p * 2 + e), tile(merged, p * 2 + e),
                                        tile(mixed_hi, p * 2 + e).bitcast(F32), ALU.subtract).then_inc(mixed_ready.sem, 1)
                out_product(l, 1, C_WO, DK // 2)
                norm(l, 2)
                ffn(l, 1, C_FFN2)
                out_product(l, 2, C_FFN2_OUT, UNITS)

        @block.tensor
        def _(pe):
            pe.sem_inc(used.sem, SLOTS)
            for b in range(8):
                pe.sem_inc(bank[b].sem, 1)

            def product(out, slot, i, rhs_hi, rhs_lo, start, stop):
                nc.tensor.matmul(out, whi[slot][:, i, :], rhs_hi, start=start, stop=False)
                nc.tensor.matmul(out, whi[slot][:, i, :], rhs_lo, start=False, stop=False)
                return nc.tensor.matmul(out, wlo[slot][:, i, :], rhs_hi, start=False, stop=stop)

            def carry_waits():
                pe.sem_inc(waits_carried.sem, 1)

            def norm_total(l, s):
                pe.wait_ge(square_summed.sem, square_summed(l, s * DK))
                nc.tensor.matmul(ps[4][:], ones, tmp[2][:], start=True, stop=True).then_inc(norm_sum.sem, 1)

            def ffn(l, f, s, c0):
                def unit(u, first=False, sums=(False, False)):
                    for p in range(2):
                        c = c0 + 2 * p
                        pe.wait_ge(bank[2 * p].sem, bank[2 * p].before(l, f"ffn{f}", u))
                        pe.wait_ge(bank[2 * p + 1].sem, bank[2 * p + 1].before(l, f"ffn{f}", u))
                        pe.wait_ge(split.sem, split(l, u * 4 + (c + 2)))
                        for k in range(DK):
                            if first and p == 0:
                                pe.wait_ge(h_ready.sem, h_ready(l, s * DK + k + 1))
                            for side in range(2):
                                mm = product(ps[2 * p + side][:], (c + side) % SLOTS, k, h_hi[:, k, :], h_lo[:, k, :],
                                             k == 0, k == DK - 1)
                                if k == DK - 1:
                                    mm.then_inc(used.sem, 1)
                        if sums[p]:
                            ada_total(u * 2 + (p - 1))

                def ada_total(h):
                    pe.wait_ge(ada_free.sem, ada_free(l, (h + 1) * PIECES))
                    for m in range(4):
                        mm = nc.tensor.matmul(ps[7][:, m:m + 1], ada_acc[:, P * m:P * m + P], ones[:, 0:1],
                                              start=True, stop=True)
                    mm.then_inc(ada_sum.sem, 1)

                if f == 0:
                    unit(0, True, (False, True))
                    with loop(ENG.PE, 1, ADA_STEP) as u:
                        unit(u, sums=(True, True))
                    unit(ADA_STEP, sums=(True, False))
                    unit(ADA_STEP + 1)
                else:
                    unit(0, True)
                    with loop(ENG.PE, 1, UNITS) as u:
                        unit(u)

            def out_product(l, s, c0, n, ready, ready_at, rhs_hi, rhs_lo):
                for half in range(2):
                    banks = [4 * (1 - half) + i for i in range(4)]
                    for b in banks:
                        pe.wait_ge(bank[b].sem, bank[b].before(l, f"out{s}"))

                    def chunk(k, c, c_static, first=False, last=False):
                        pe.wait_ge(split.sem, split(l, c + 1))
                        if half == 0:
                            pe.wait_ge(ready.sem, ready(l, ready_at + k + 2))
                        order = [(kk, i) for kk in range(2) for i in range(4)]
                        if last:
                            order = [(kk, i) for i in range(4) for kk in range(2)]
                        for kk, i in order:
                            mm = product(ps[banks[i]][:], c_static % SLOTS, 4 * kk + i, tile(rhs_hi, k + kk),
                                         tile(rhs_lo, k + kk), first and kk == 0, last and kk == 1)
                            if last and kk == 1 and i < 3:
                                mm.then_inc(out_tile.sem, 1)
                        mm.then_inc(used.sem, 1)

                    c = c0 + half * n
                    chunk(0, c, c, first=True)
                    loops = (n - 2) // SLOTS
                    if loops > 1:
                        with loop(ENG.PE, 0, loops) as u:
                            for j in range(SLOTS):
                                chunk(u * 8 + (2 + 2 * j), u * 4 + (c + 1 + j), c + 1 + j)
                    else:
                        loops = 0
                    for j in range(1 + SLOTS * loops, n - 1):
                        chunk(2 * j, c + j, c + j)
                    chunk(2 * (n - 1), c + n - 1, c + n - 1, last=True)

            pe.wait_ge(cond_ready.sem, 1)
            pe.wait_ge(ada_first_loaded.sem, 16 * 2 * ADA_FIRST)
            for g in range(ADA_FIRST):
                for m in range(DK):
                    for k in range(DK):
                        mm = nc.tensor.matmul(ps[7][:, g * DK + m:g * DK + m + 1], ada_now[g][:, k, P * m:P * m + P],
                                              cond[:, k:k + 1], start=(k == 0), stop=(k == DK - 1))
            mm.then_inc(ada_first_ready.sem, 1)
            pe.wait_ge(x_loaded.sem, 32)

            with loop(ENG.PE, 0, LAYERS) as l:
                norm_total(l, 0)
                ffn(l, 0, 0, C_FFN1)
                pe.wait_ge(mods_done.sem, mods_done(l, HALVES))
                out_product(l, 0, C_FFN1_OUT, UNITS, act_ready, 0, act_hi, act_lo)
                norm_total(l, 1)

                def proj(j, c, c_static, phase, time, first=False):
                    b, slot = j % 4, c_static % SLOTS
                    pe.wait_ge(bank[b].sem, bank[b].before(l, phase, time))
                    pe.wait_ge(split.sem, split(l, c + 1))
                    for k in range(DK):
                        if first:
                            pe.wait_ge(h_ready.sem, h_ready(l, DK + k + 1))
                        mm = product(ps[b][:], slot, k, h_hi[:, k, :], h_lo[:, k, :], k == 0, k == DK - 1)
                    mm.then_inc(used.sem, 1)

                for j in range(4):
                    proj(j, C_PROJ + j, C_PROJ + j, "proj", 0, first=(j == 0))
                with loop(ENG.PE, 1, 5) as u:
                    for j in range(4):
                        proj(j, u * 4 + (C_PROJ + j), C_PROJ + j, "proj", u)

                def head_norm(n):
                    b = NORM_BANK[n]
                    pe.wait_ge(bank[b].sem, bank[b].before(l, f"norm{n}"))
                    pe.wait_ge(qk_square.sem, qk_square(l, n + 1))
                    nc.tensor.matmul(ps[b][:], head_ones, tmp[n % 2][:], start=True, stop=True).then_inc(qk_norm.sem, 1)

                def turn(n):
                    b = ROPE_BANK[n]
                    pe.wait_ge(bank[b].sem, bank[b].before(l, f"rope{n}"))
                    pe.wait_ge(qk_normed.sem, qk_normed(l, n + 1))
                    nc.tensor.matmul(ps[b][:], half_turn, k_pad[:, CHUNK:] if n == 0 else tile(q, n - 1),
                                     start=True, stop=True).then_inc(qk_turned.sem, 1)

                def turn_v():
                    pe.wait_ge(bank[J_V % 4].sem, bank[J_V % 4].after(l, "proj", J_V // 4))
                    for b in (4, 5):
                        pe.wait_ge(bank[b].sem, bank[b].before(l, "v_turn"))
                    for ch in range(NCH):
                        mm = nc.tensor.transpose(ps[4 + ch // 4][:, (ch % 4) * P:(ch % 4 + 1) * P],
                                                 v_pad[:, CHUNK * ch:CHUNK * ch + P], ident)
                    mm.then_inc(v_turned.sem, 1)

                pe.wait_ge(pads_ready.sem, pads_ready(l, 1))
                for j in range(J_K, PROJ_TILES):
                    phase, time = ("proj", j // 4) if j < 28 else ("proj_tail", 0)
                    proj(j, C_PROJ + j, C_PROJ + j, phase, time)
                    if 22 <= j < 27:
                        head_norm(j - 22)
                    if j >= 25:
                        if j == 28:
                            turn_v()
                        if j < 29:
                            turn(j - 25) if j != 28 else turn(3)
                turn(4)

                def gate(c, c_static, b, phase, time=0):
                    pe.wait_ge(bank[b].sem, bank[b].before(l, phase, time))
                    pe.wait_ge(split.sem, split(l, c + 1))
                    for k in range(DK):
                        mm = product(ps[b][:], c_static % SLOTS, k, h_hi[:, k, :], h_lo[:, k, :], k == 0, k == DK - 1)
                    mm.then_inc(used.sem, 1)

                def pool_branch(half):
                    c = C_POOL + 5 * half
                    pe.wait_ge(pool_ready.sem, pool_ready(l, 2 * half + 2))
                    pe.wait_ge(split.sem, split(l, c + 1))
                    for i in range(4):
                        b, g = 4 + i, 2 * half + i // 2
                        pe.wait_ge(bank[b].sem, bank[b].before(l, f"pool{half}"))
                        mm = product(ps[b][:], c % SLOTS, i, pool_hi[:, g, :], pool_lo[:, g, :], True, True)
                    mm.then_inc(used.sem, 1)
                    for i in range(4):
                        if half == 1 and i == 3:
                            pe.wait_ge(xc_ready.sem, xc_ready(l, 4))
                        gate(c + 1 + i, c + 1 + i, i, f"pool{half}")

                pool_branch(0)
                pe.wait_ge(bank[3].sem, bank[3].before(l, "pool1"))
                pe.wait_ge(ln_sum.sem, ln_sum(l, 3))
                nc.tensor.matmul(ps[3][:], ones, pair[1][:], start=True, stop=True).then_inc(ln_mean.sem, 1)
                pool_branch(1)
                pe.wait_ge(bank[3].sem, bank[3].before(l, "sc"))
                pe.wait_ge(xc_summed.sem, xc_summed(l, 4))
                nc.tensor.matmul(ps[3][:], ones, pair[1][:], start=True, stop=True).then_inc(ln_var.sem, 1)

                def own(c, c_static, b, phase, time, rhs_hi, rhs_lo):
                    pe.wait_ge(bank[b].sem, bank[b].before(l, phase, time))
                    pe.wait_ge(split.sem, split(l, c + 1))
                    for k in range(4):
                        mm = product(ps[b][:], c_static % SLOTS, k, rhs_hi[:, k, :], rhs_lo[:, k, :], k == 0, k == 3)
                    mm.then_inc(used.sem, 1)

                def scores(p):
                    pe.wait_ge(q_now_ready.sem, q_now_ready(l, p + 1))
                    for b in (4, 5):
                        pe.wait_ge(bank[b].sem, bank[b].before(l, "sc", p))
                    carry_waits()
                    for ch in range(NCH):
                        for g in range(2):
                            rows = slice(HD * g, HD * g + HD)
                            mm = nc.tensor.matmul(ps[4 + ch // 4][rows, (ch % 4) * P:(ch % 4 + 1) * P],
                                                  q_now[rows, CHUNK * ch:CHUNK * ch + CHUNK],
                                                  k_pad[rows, CHUNK * ch:CHUNK * ch + P], start=True, stop=True)
                    mm.then_inc(scores_ready.sem, 1)

                def turn_probs(p):
                    pe.wait_ge(probs_ready.sem, probs_ready(l, p + 1))
                    for b in (6, 7):
                        pe.wait_ge(bank[b].sem, bank[b].before(l, "sc", p))
                    for ch in range(NCH):
                        mm = nc.tensor.transpose(ps[6 + ch // 4][:, (ch % 4) * P:(ch % 4 + 1) * P],
                                                 probs[:, ch, :], ident)
                    mm.then_inc(probs_turned.sem, 1)

                pe.wait_ge(sc_ready.sem, sc_ready(l, 4))
                pe.wait_ge(qk_ready.sem, qk_ready(l, 5))
                pe.wait_ge(k_first.sem, k_first(l, 1))
                pe.wait_ge(ln_rms.sem, ln_rms(l, 1))
                carry_waits()
                with loop(ENG.PE, 0, 4) as p:
                    c = p * 4 + C_SC
                    gate(c, C_SC, 0, "sc", p)
                    scores(p)
                    own(c + 1, C_SC + 1, 1, "sc", p, sc_hi, sc_lo)
                    gate(c + 2, C_SC + 2, 2, "sc", p)
                    own(c + 3, C_SC + 3, 3, "sc", p, sc_hi, sc_lo)
                    turn_probs(p)
                for b in (4, 5, 6, 7):
                    pe.wait_ge(bank[b].sem, bank[b].before(l, "pv"))
                for ch in range(NCH):
                    for g in range(2):
                        cols = (ch % 2) * QT * CHUNK
                        mm = nc.tensor.matmul(ps[4 + ch // 2][HD * g:HD * g + HD, cols:cols + QT * CHUNK],
                                              v_tok[:, ch, HD * g:HD * g + HD],
                                              probs_t[:, ch, g, :, :].rearrange("p i t -> p (i t)"),
                                              start=True, stop=True)
                mm.then_inc(pv_ready.sem, 1)

                def branch(name, c0, rhs_hi, rhs_lo):
                    with loop(ENG.PE, 0, 4) as p:
                        for e in range(2):
                            c = p * 4 + (c0 + 2 * e)
                            gate(c, c0 + 2 * e, 2 * e, name, p)
                            own(c + 1, c0 + 2 * e + 1, 2 * e + 1, name, p, rhs_hi, rhs_lo)

                pe.wait_ge(conv_ready.sem, conv_ready(l, 4))
                carry_waits()
                branch("conv", C_CONV, conv_hi, conv_lo)
                for b in (4, 5, 6, 7):
                    pe.wait_ge(bank[b].sem, bank[b].after(l, "pv"))
                carry_waits()
                branch("attn", C_ATTN, o_hi, o_lo)
                out_product(l, 1, C_WO, DK // 2, mixed_ready, 0, mixed_hi, mixed_lo)
                norm_total(l, 2)
                ffn(l, 1, 2, C_FFN2)
                out_product(l, 2, C_FFN2_OUT, UNITS, act_ready, FK, act_hi, act_lo)


def _lay_out(inputs):
    f = {k: np.asarray(v) for k, v in inputs.items()}
    heads = [h for i in range(QT) for h in (i, i + QT)]

    def in_chunk(w, m):
        return w[:, m * P:m * P + P].reshape(-1, P, P).transpose(1, 0, 2)

    def out_chunk(w, half, c):
        return w.reshape(-1, P, 2, 4, P)[2 * c:2 * c + 2, :, half].transpose(1, 0, 2, 3).reshape(P, 8, P)

    def ffn_chunks(wi, wo):
        for n in range(FK):
            yield in_chunk(wi, n)
            yield in_chunk(wi, FK + n)
        for half in range(2):
            for c in range(FK // 2):
                yield out_chunk(wo, half, c)

    full, half, par = [], [], []
    for l in range(LAYERS):
        full += ffn_chunks(f["ffn1_wi"][l], f["ffn1_wo"][l])
        w = f["w_in"][l]
        cuts = np.cumsum([512, 128, 128, 512, 512, 512, 512, 512])
        wq, wk, wv, wu, wa, wg, wb, wc, wx = np.split(w, cuts, axis=1)
        wq = wq.reshape(D, 8, HD)[:, heads].reshape(D, 512)
        for i in range(4):
            full += [in_chunk(t, i) for t in (wa, wg, wc, wx, wb)]
        full += [in_chunk(wk, 0)] + [in_chunk(wq, i) for i in range(4)] + [in_chunk(wv, 0)]
        full += [in_chunk(wu, i) for i in range(4)]
        gates = [f["w_gate"][l][:, b * D:b * D + D] for b in range(4)]
        for hf in range(2):
            ms = range(4 * hf, 4 * hf + 4)
            half.append(np.stack([f["pool_w"][l, m // 2][:, (m % 2) * P:(m % 2) * P + P] for m in ms], axis=1))
            full += [in_chunk(gates[1], m) for m in ms]
        attn_wo = f["attn_wo"][l].reshape(8, HD, D)[heads].reshape(512, D)
        for b, own in ((3, f["sc_wo"][l]), (2, f["conv_wo"][l]), (0, attn_wo)):
            for m in range(DK):
                full.append(in_chunk(gates[b], m))
                half.append(in_chunk(own, m))
        full += [out_chunk(f["w_o"][l], hf, c) for hf in range(2) for c in range(4)]
        full += ffn_chunks(f["ffn2_wi"][l], f["ffn2_wo"][l])

        def cols(a):
            return a.reshape(-1, P).T

        sinks = f["attn_sinks"][l]
        par.append(np.concatenate([
            cols(f["ffn1_norm"][l]), cols(f["mix_norm"][l]), cols(f["ffn2_norm"][l]), cols(f["b_gate"][l]),
            cols(f["pool_scale"][l]),
            f["conv_dw"][l].reshape(TAPS, 4, P).transpose(2, 1, 0).reshape(P, 4 * TAPS), cols(f["conv_db"][l]),
            cols(f["conv_ln_g"][l]), cols(f["conv_ln_b"][l]),
            f["sc_w"][l].reshape(SC_TAPS, 4, P).transpose(2, 1, 0).reshape(P, 4 * SC_TAPS),
            np.tile(f["q_norm"][l], 2)[:, None], np.tile(f["k_norm"][l], 2)[:, None],
            np.repeat(sinks.reshape(2, QT), HD, axis=0)], axis=1))
    out = {"full": np.stack(full), "half": np.stack(half), "par": np.stack(par)}
    assert out["full"].shape[0] == LAYERS * N_FULL and out["half"].shape[0] == LAYERS * N_HALF

    ada = f["ada_w"].reshape(LAYERS, DK, P, MODS, D).transpose(0, 3, 2, 1, 4).reshape(LAYERS * MODS, P, DK, D)
    spare = ADA_GROUPS - LAYERS * MODS
    out["ada_first"] = ada[:ADA_FIRST]
    rest = np.concatenate([ada[ADA_FIRST:], np.zeros((spare, P, DK, D), ada.dtype)])
    out["ada_rest"] = rest.reshape(-1, P, PIECES, 2, 2, T).transpose(0, 4, 2, 1, 3, 5).reshape(-1, P, 2, T)
    ada_b = np.concatenate([f["ada_b"].reshape(-1), np.zeros(spare * D, ada.dtype)]).reshape(-1, P).T
    freq = (10000.0 ** (-np.arange(0, HD, 2, dtype=np.float32) / HD)).astype(np.float32)
    count = np.stack([w / np.minimum(np.arange(1, UPAD + 1), w) for w in WINDOWS]).astype(np.float32).reshape(1, -1)
    out["glob"] = np.concatenate([ada_b, f["c"].reshape(DK, P).T, np.tile(freq, 4)[:, None],
                                  np.repeat(count, P, axis=0)], axis=1)
    out["positions"] = np.broadcast_to(f["positions"].reshape(1, T), (P, T))
    out["x"] = f["x"].reshape(T, DK, P).transpose(2, 1, 0)
    i = np.arange(P)
    turn = np.zeros((P, P), np.float32)
    low = i[i % HD < HD // 2]
    turn[low + HD // 2, low] = -1.0
    turn[low, low + HD // 2] = 1.0
    out["mats"] = np.stack([np.ones((P, P), np.float32), (i[:, None] // HD == i // HD).astype(np.float32), turn,
                            np.eye(P, dtype=np.float32)], axis=1)
    return {k: np.ascontiguousarray(v) for k, v in out.items()}


def kernel(**inputs):
    import concourse.bacc as bacc
    from concourse.bass_utils import run_bass_kernel_spmd

    arrays = _lay_out(inputs)
    nc = bacc.Bacc("TRN2", target_bir_lowering=False, num_devices=1)
    io = {name: nc.dram_tensor(name + "_in", a.shape, mybir.dt.from_np(a.dtype), kind="ExternalInput").ap()
          for name, a in arrays.items()}
    io["rope_scratch"] = nc.dram_tensor("rope_scratch", (P, 2, T), F32).ap()
    io["out"] = nc.dram_tensor("out_x", (P, DK, T), F32, kind="ExternalOutput").ap()
    trunk_program(nc, io)
    r = run_bass_kernel_spmd(nc, [{name + "_in": a for name, a in arrays.items()}], core_ids=[0])
    return r.results[0]["out_x"].transpose(2, 1, 0).reshape(1, T, D)
```

```python
from contextlib import ExitStack

import numpy as np
import concourse.bass as bass
from concourse import mybir

F32 = mybir.dt.float32
F32R = mybir.dt.float32r
I32 = mybir.dt.int32
ACT = mybir.ActivationFunctionType
ALU = mybir.AluOpType
AX = mybir.AxisListType
ENG = mybir.EngineType

P = 128
LAYERS = 2
T = 512
D = 1024
DK = D // P
FFN = 2816
FK = FFN // P
UNITS = FK // 2
EPS = 1e-6
HD = 64
CHUNK = 64
NCH = T // CHUNK
QT = 4
TAPS = 31
SC_TAPS = 3
WINDOWS = (2, 4, 8, 16)
UPAD = 16
MODS = 9

TOKENS = {None: slice(0, T), 0: slice(0, T // 2), 1: slice(T // 2, T)}
STEPS = [(m, None) for m in range(4)] + [(m, t) for t in range(2) for m in range(4, DK)]
SUMS = STEPS[1:]

OUT_TILES = len(STEPS) - 2


def through(steps, m, t):
    return steps.index((m, t)) + 1


def replaced(m, t):
    return through(SUMS, max(1, m - 2), t if m >= 6 else None)


C_FFN1 = 0
C_FFN1_OUT = C_FFN1 + 2 * FK
C_PROJ = C_FFN1_OUT + FK
PROJ_TILES = 30
C_POOL = C_PROJ + PROJ_TILES
C_SC = C_POOL + 10
C_CONV = C_SC + 16
C_ATTN = C_CONV + 16
C_WO = C_ATTN + 16
C_FFN2 = C_WO + DK
C_FFN2_OUT = C_FFN2 + 2 * FK
CHUNKS = C_FFN2_OUT + FK
SLOTS = 4
assert CHUNKS % SLOTS == 0 and C_PROJ % SLOTS == 2 and C_SC % SLOTS == 2

ADA_FIRST = 2
ADA_STEP = 9
ADA_GROUPS = ADA_FIRST + LAYERS * ADA_STEP
HALVES = 2 * ADA_STEP
PIECES = 4

PAR = {}
_at = 0
for _name, _n in (("gain", 3 * DK), ("b_gate", 4 * DK), ("pool_scale", DK), ("conv_w", 4 * TAPS), ("conv_b", 4),
                  ("ln_g", 4), ("ln_b", 4), ("sc_w", 4 * SC_TAPS), ("q_gain", 1), ("k_gain", 1), ("sink", QT)):
    PAR[_name] = _at
    _at += _n
NPAR = _at
G_ADA_B = 0
G_C = ADA_GROUPS * DK
G_FREQ = G_C + DK
G_COUNT = G_FREQ + 1
NGLOBAL = G_COUNT + len(WINDOWS) * UPAD

TWO_PI = 6.283185307179586
TURN_MID = 2029 / 2 ** 20
TURN = (6.28125, TURN_MID, TWO_PI - 6.28125 - TURN_MID)
ROUND = 12582912.0

J_K, J_Q, J_V, J_U = 20, 21, 25, 26

USES = (
    ("ffn0", UNITS, (0, 1, 2, 3)),
    ("out0", 0, range(8)),
    ("proj", PROJ_TILES // 4, (0, 1, 2, 3)),
    ("proj_tail", 1, (0, 1)),
    ("norm0", 1, (4,)), ("norm1", 1, (5,)), ("norm2", 1, (4,)),
    ("norm3", 1, (5,)), ("rope0", 1, (6,)), ("norm4", 1, (4,)), ("rope1", 1, (7,)),
    ("rope2", 1, (6,)), ("v_turn", 1, (4, 5)), ("rope3", 1, (7,)), ("rope4", 1, (6,)),
    ("pool0", 1, range(8)),
    ("pool1", 1, range(8)),
    ("sc", 4, range(8)),
    ("pv", 1, (4, 5, 6, 7)),
    ("conv", 4, (0, 1, 2, 3)),
    ("attn", 4, (0, 1, 2, 3)),
    ("out1", 0, range(8)),
    ("ffn1", UNITS, (0, 1, 2, 3)),
    ("out2", 0, range(8)),
)
FIRST_USE, USES_OF = {}, [0] * 8
for _name, _times, _banks in USES:
    for _b in _banks:
        FIRST_USE[_name, _b] = USES_OF[_b]
        USES_OF[_b] += _times
TOTAL_BANK, RMS_BANK = ((3, 4), (3, 4), (4, 4)), ((2, 5), (2, 5), (5, 5))
NORM_BANK, ROPE_BANK = (4, 5, 4, 5, 4), (6, 7, 6, 7, 6)

def tiles_of(c):
    if C_POOL <= c < C_SC:
        return 4 if (c - C_POOL) % 5 == 4 else 8
    return 4 if C_SC <= c < C_WO and (c - C_SC) % 2 else 8


N_HALF = sum(tiles_of(c) == 4 for c in range(CHUNKS))
N_FULL = CHUNKS - N_HALF


class Signal:

    def __init__(self, nc, ctx, name, per_layer=0, start=0):
        self.sem = ctx.enter_context(nc.semaphore(name))
        self.per_layer, self.start = per_layer, start

    def __call__(self, l, n):
        return l * self.per_layer + (n + self.start)


class Bank(Signal):

    def __init__(self, nc, ctx, b):
        super().__init__(nc, ctx, f"bank_free{b}", USES_OF[b], 1)
        self.b = b

    def before(self, l, phase, time=0):
        return self(l, time + FIRST_USE[phase, self.b])

    def after(self, l, phase, time=0):
        return self(l, time + (FIRST_USE[phase, self.b] + 1))


def trunk_program(nc, io):
    ctx = ExitStack()
    with ctx:
        place = [(nc.sbuf_base + 31) // 32 * 32]

        def sb(name, shape, dt=F32):
            at = place[0]
            place[0] += (4 * int(np.prod(shape[1:])) + 31) // 32 * 32
            return nc.alloc_sbuf_tensor_at(name, shape, dt, offset=at)

        raw = [sb(f"weights_raw{s}", [P, 8, P]) for s in range(SLOTS)]
        whi = [sb(f"weights_hi{s}", [P, 8, P], F32R) for s in range(SLOTS)]
        wlo = [sb(f"weights_lo{s}", [P, 8, P], F32R) for s in range(SLOTS)]
        x = sb("x", [P, DK, T])
        h_hi = sb("h_hi", [P, DK, T], F32R)
        h_lo = sb("h_lo", [P, DK, T], F32R)
        tmp = [sb(f"tmp{i}", [P, T]) for i in range(4)]
        mats = sb("mats", [P, 4, P])
        ones, head_ones, half_turn, ident = (mats[:, i, :] for i in range(4))
        glob = sb("glob", [P, NGLOBAL])
        par = sb("par", [P, NPAR])
        mods = sb("mods", [P, ADA_GROUPS * DK])
        cond = sb("cond", [P, DK])
        eps = sb("eps", [P, 1])
        table_load = sb("table_load", [P, 1])
        mod_gain = sb("mod_gain", [P, DK])
        mod_shift = sb("mod_shift", [P, DK])
        mod_gate = sb("mod_gate", [P, DK])
        neg_sink = sb("neg_sink", [P, QT])
        soft = sb("soft", [P, 5, NCH])

        region, REGION_KB = place[0], 98

        def at(name, kb, shape, dt=F32):
            assert kb * 1024 + 4 * np.prod(shape[1:]) <= REGION_KB * 1024
            return nc.alloc_sbuf_tensor_at(name, shape, dt, offset=region + int(kb * 1024))

        act_hi = at("act_hi", 0, [P, FK * T], F32R)
        act_lo = at("act_lo", 44, [P, FK * T], F32R)
        ada_buf = [at(f"ada_buf{b}", 88 + 4 * b, [P, 2, T]) for b in range(2)]
        ada_acc = at("ada_acc", 96, [P, T])
        ada_now = [at(f"ada_now{g}", 32 * g, [P, DK, D]) for g in range(ADA_FIRST)]
        angle = [at(f"angle{i}", 64 + 2 * i, [P, T]) for i in range(4)]
        angle_i = at("angle_i", 72, [P, T], I32)
        ada_total = [at(f"ada_total{g}", 74 + 4 * g, [P, D]) for g in range(ADA_FIRST)]
        sc_hi, sc_lo = at("sc_hi", 0, [P, 4, T], F32R), at("sc_lo", 8, [P, 4, T], F32R)
        u_pad = [at(f"u_pad{g}", 16 + 2.125 * g, [P, UPAD + T]) for g in range(4)]
        window = [at(f"window{i}", 24.5 + 2.125 * i, [P, UPAD + T]) for i in range(2)]
        z_pad = [at(f"z_pad{i}", 32 + 2.125 * i, [P, TAPS - 1 + T]) for i in range(2)]
        s_pad = at("s_pad", 36.5, [P, SC_TAPS - 1 + T])
        s_conv = at("s_conv", 38.75, [P, T])
        sc_out = at("sc_out", 40.75, [P, T])
        odd_taps = at("odd_taps", 42.75, [P, T])
        pool_hi, pool_lo = at("pool_hi", 48, [P, 4, T], F32R), at("pool_lo", 56, [P, 4, T], F32R)
        q = at("q", 64, [P, QT * T])
        k_pad = at("k_pad", 72, [P, CHUNK + T])
        v_pad = at("v_pad", 74.25, [P, CHUNK + T])
        v_tok = at("v_tok", 76.5, [P, NCH, P])
        rope_tab = at("rope_tab", 80.5, [P, 2, T])
        conv_out = [at(f"conv_out{i}", 88.5 + 2 * i, [P, T]) for i in range(4)]
        pair = [at("pair0", 42.75, [P, T]), at("pair1", 86.5, [P, T])]
        conv_hi, conv_lo = at("conv_hi", 16, [P, 4, T], F32R), at("conv_lo", 24, [P, 4, T], F32R)
        merged = at("merged", 32, [P, DK * T])
        xc_sq = [at(f"xc_sq{i}", 80.5 + 2 * i, [P, T]) for i in range(2)]
        probs = at("probs", 84.5, [P, NCH, P])
        probs_t = at("probs_t", 48, [P, NCH, 2, QT, CHUNK])
        o_hi, o_lo = at("o_hi", 48, [P, QT, T], F32R), at("o_lo", 56, [P, QT, T], F32R)
        mixed_hi, mixed_lo = at("mixed_hi", 0, [P, DK * T], F32R), at("mixed_lo", 16, [P, DK * T], F32R)
        q_now = tmp[3]

        ps = [ctx.enter_context(nc.psum_tensor(f"bank{b}", [P, T], F32)) for b in range(8)]

        def sig(name, per_layer=0, start=0):
            return Signal(nc, ctx, name, per_layer, start)

        loaded = [sig(f"loaded{s}", 16 * (CHUNKS // SLOTS)) for s in range(SLOTS)]
        hi_done = sig("hi_done", CHUNKS)
        split = sig("split", CHUNKS, SLOTS)
        used = sig("used", CHUNKS, SLOTS)
        bank = [Bank(nc, ctx, b) for b in range(8)]
        x_loaded = sig("x_loaded")
        glob_loaded = sig("glob_loaded")
        ada_first_loaded = [sig(f"ada_first_loaded{i}") for i in range(ADA_FIRST * DK // 2)]
        ada_first_begun = sig("ada_first_begun")
        ada_first_summed = sig("ada_first_summed")
        par_loaded = sig("par_loaded", 16)
        rope_loaded = sig("rope_loaded", 16)
        ada_loaded = [sig(f"ada_loaded{b}", 16 * (HALVES * PIECES // 2)) for b in range(2)]
        ada_free = sig("ada_free", HALVES * PIECES, 2)
        rope_stored = sig("rope_stored")
        out_stored = sig("out_stored")
        setup_step = sig("setup_step")
        angles_ready = sig("angles_ready")
        angle_sin = sig("angle_sin")
        cond_ready = sig("cond_ready")
        ada_first_ready = sig("ada_first_ready")
        ada_step = sig("ada_step", HALVES * PIECES)
        ada_sum = sig("ada_sum", HALVES)
        mods_done = sig("mods_done", HALVES, 1)
        coef_ready = sig("coef_ready", 3)
        gate_coef = sig("gate_coef", 3)
        square_ready = sig("square_ready", 3 * len(STEPS), len(STEPS))
        square_summed = sig("square_summed", 3 * len(SUMS), len(SUMS))
        norm_sum = sig("norm_sum", 3 * 2)
        rms_ready = sig("rms_ready", 3 * 2)
        inv_rms = sig("inv_rms", 3 * 2)
        xn_ready = sig("xn_ready", 3 * 2 * DK)
        h_hi_ready = sig("h_hi_ready", 3 * 2 * DK)
        h_whole = sig("h_whole", 3 * DK)
        h_ready = sig("h_ready", 3 * 2 * DK)
        act_hi_ready = sig("act_hi_ready", 2 * FK)
        act_ready = sig("act_ready", 2 * FK)
        out_tile = sig("out_tile", 3 * OUT_TILES)
        x_updated = sig("x_updated", 3 * len(STEPS), len(STEPS))
        x_begun = sig("x_begun", 2 * 4)
        pads_ready = sig("pads_ready", 1)
        conv_tap = sig("conv_tap", 4 * (TAPS + 1))
        sc_tap = sig("sc_tap", 4 * SC_TAPS)
        sc_out_ready = sig("sc_out_ready", 4)
        sc_hi_ready = sig("sc_hi_ready", 4)
        sc_ready = sig("sc_ready", 4)
        qk_square = sig("qk_square", 5)
        qk_norm = sig("qk_norm", 5)
        qk_inv = sig("qk_inv", 5)
        qk_normed = sig("qk_normed", 5)
        qk_turned = sig("qk_turned", 5)
        rope_part = sig("rope_part", 5)
        qk_ready = sig("qk_ready", 5)
        k_first = sig("k_first", 1)
        v_turned = sig("v_turned", 1)
        window_step = sig("window_step", 14)
        pool_out = sig("pool_out", 4)
        pool_hi_ready = sig("pool_hi_ready", 4)
        pool_ready = sig("pool_ready", 4)
        ln_sum = sig("ln_sum", 3)
        ln_mean = sig("ln_mean", 1)
        xc_ready = sig("xc_ready", 4)
        xc_square = sig("xc_square", 4)
        xc_summed = sig("xc_summed", 4)
        ln_var = sig("ln_var", 1)
        ln_rms = sig("ln_rms", 1)
        ln_inv = sig("ln_inv", 1)
        ln_y = sig("ln_y", 4)
        conv_silu = sig("conv_silu", 4)
        conv_ready = sig("conv_ready", 4)
        merged_ready = sig("merged_ready", 3 * DK, 1)
        q_now_ready = sig("q_now_ready", QT)
        scores_ready = sig("scores_ready", QT)
        max_found = sig("max_found", QT)
        neg_max = sig("neg_max", QT)
        exp_ready = sig("exp_ready", QT)
        total_ready = sig("total_ready", 2 * QT)
        probs_ready = sig("probs_ready", QT)
        probs_turned = sig("probs_turned", QT)
        pv_ready = sig("pv_ready", 1)
        waits_carried = sig("waits_carried")
        o_hi_ready = sig("o_hi_ready", 4)
        mixed_hi_ready = sig("mixed_hi_ready", DK)
        mixed_ready = sig("mixed_ready", DK)

        def loop(engine, first, last):
            return nc.Fori(first, last, engines=(engine,), hint_back_edge=True)

        def tile(flat, i):
            return flat[:, bass.ds(i * T, T)]

        def mod_cols(l, which):
            return mods[:, bass.ds(l * (MODS * DK) + which * DK, DK)]

        def par_col(name, i=0):
            return par[:, bass.ds(i + PAR[name], 1)]

        block = ctx.enter_context(nc.Block())

        @block.sync
        def _(sp):
            sp.dma_start(glob[:], io["glob"]).then_inc(glob_loaded.sem, 16)
            sp.dma_start(angle_i[:], io["positions"]).then_inc(glob_loaded.sem, 16)
            sp.dma_start(mats[:], io["mats"]).then_inc(x_loaded.sem, 16)
            sp.dma_start(x[:], io["x"]).then_inc(x_loaded.sem, 16)
            for g in range(ADA_FIRST):
                for i in range(DK // 2):
                    sp.dma_start(ada_now[g][:, 2 * i:2 * i + 2, :], io["ada_first"][g, i]
                                 ).then_inc(ada_first_loaded[4 * g + i].sem, 16)

            def load(l, c, slot, full=None, half=None):
                sp.wait_ge(split.sem, split(l, c + (1 - SLOTS)))
                if half is None:
                    sp.dma_start(raw[slot][:], io["full"][l * N_FULL + full]).then_inc(loaded[slot].sem, 16)
                else:
                    sp.dma_start(raw[slot][:, 0:4, :], io["half"][l * N_HALF + half]).then_inc(loaded[slot].sem, 16)

            with loop(ENG.SP, 0, LAYERS) as l:
                for c in range(SLOTS):
                    load(l, c, c, c)
                sp.dma_start(par[:], io["par"][l]).then_inc(par_loaded.sem, 16)
                for c in range(SLOTS, 2 * SLOTS):
                    load(l, c, c % SLOTS, c)
                with loop(ENG.SP, 0, ADA_STEP) as u:
                    for j in range(SLOTS):
                        for b in range(2):
                            piece = u * 8 + (2 * j + b)
                            sp.wait_ge(ada_free.sem, ada_free(l, piece - 1))
                            sp.dma_start(ada_buf[b][:], io["ada_rest"][l * (HALVES * PIECES) + piece]
                                         ).then_inc(ada_loaded[b].sem, 16)
                        load(l, u * 4 + (2 * SLOTS + j), j, u * 4 + (2 * SLOTS + j))
                with loop(ENG.SP, ADA_STEP + 2, 20) as u:
                    for j in range(SLOTS):
                        load(l, u * 4 + j, j, u * 4 + j)
                sp.wait_ge(h_ready.sem, h_ready(l, 3 * DK + 1))
                sp.wait_ge(rope_stored.sem, 32)
                sp.dma_start(rope_tab[:], io["rope_scratch"]).then_inc(rope_loaded.sem, 16)
                with loop(ENG.SP, 20, C_POOL // SLOTS) as u:
                    for j in range(SLOTS):
                        load(l, u * 4 + j, j, u * 4 + j)
                full, half = C_POOL, 0
                for c in range(C_POOL, C_SC):
                    if tiles_of(c) == 4:
                        load(l, c, c % SLOTS, half=half)
                        half += 1
                    else:
                        load(l, c, c % SLOTS, full)
                        full += 1
                with loop(ENG.SP, 0, (C_WO - C_SC) // SLOTS) as u:
                    for j in range(SLOTS):
                        if j % 2:
                            load(l, u * 4 + (C_SC + j), (C_SC + j) % SLOTS, half=u * 2 + (half + j // 2))
                        else:
                            load(l, u * 4 + (C_SC + j), (C_SC + j) % SLOTS, u * 2 + (full + j // 2))
                full += (C_WO - C_SC) // 2
                rest = CHUNKS - C_WO
                with loop(ENG.SP, 0, rest // SLOTS) as u:
                    for j in range(SLOTS):
                        load(l, u * 4 + (C_WO + j), (C_WO + j) % SLOTS, u * 4 + (full + j))
                for j in range(rest // SLOTS * SLOTS, rest):
                    load(l, C_WO + j, (C_WO + j) % SLOTS, full + j)
            for m, t in STEPS:
                sp.wait_ge(x_updated.sem, x_updated(LAYERS - 1, 2 * len(STEPS) + through(STEPS, m, t)))
                sp.dma_start(io["out"][:, m, TOKENS[t]], x[:, m, TOKENS[t]]).then_inc(out_stored.sem, 16)
            sp.wait_ge(out_stored.sem, 16 * len(STEPS))

        @block.gpsimd
        def _(pool):
            pool.sem_inc(split.sem, SLOTS)
            for m, t in SUMS[:7]:
                pool.wait_ge(square_ready.sem, through(STEPS, m, t))
                if m >= 2:
                    pool.wait_ge(square_summed.sem, through(SUMS, m, t) - 1)
                nc.gpsimd.tensor_tensor(tmp[2][:, TOKENS[t]], tmp[0 if m == 1 else 2][:, TOKENS[t]],
                                        tmp[m % 2][:, TOKENS[t]], ALU.add).then_inc(square_summed.sem, 1)

            def lo(l, c, slot, tiles=8):
                pool.wait_ge(hi_done.sem, hi_done(l, c + 1))
                nc.gpsimd.tensor_tensor(wlo[slot][:, 0:tiles, :], raw[slot][:, 0:tiles, :],
                                        whi[slot][:, 0:tiles, :].bitcast(F32), ALU.subtract).then_inc(split.sem, 1)

            with loop(ENG.Pool, 0, LAYERS) as l:
                with loop(ENG.Pool, 0, C_POOL // SLOTS) as u:
                    for j in range(SLOTS):
                        lo(l, u * 4 + j, j)
                for c in range(C_POOL, C_SC):
                    lo(l, c, c % SLOTS, tiles_of(c))
                with loop(ENG.Pool, 0, (C_WO - C_SC) // SLOTS) as u:
                    for j in range(SLOTS):
                        lo(l, u * 4 + (C_SC + j), (C_SC + j) % SLOTS, tiles_of(C_SC + j))
                rest = CHUNKS - C_WO
                with loop(ENG.Pool, 0, rest // SLOTS) as u:
                    for j in range(SLOTS):
                        lo(l, u * 4 + (C_WO + j), (C_WO + j) % SLOTS)
                for j in range(rest // SLOTS * SLOTS, rest):
                    lo(l, C_WO + j, (C_WO + j) % SLOTS)

        @block.scalar
        def _(act):
            def hi(l, c, slot, tiles=8):
                act.wait_ge(loaded[slot].sem, loaded[slot](l, (c - slot) * 4 + 16))
                act.wait_ge(used.sem, used(l, c + (1 - SLOTS)))
                nc.scalar.activation(whi[slot][:, 0:tiles, :], raw[slot][:, 0:tiles, :],
                                     ACT.Copy).then_inc(hi_done.sem, 1)

            def squares(l, s, steps):
                for m, t in steps:
                    act.wait_ge(x_updated.sem, x_updated(l, s * len(STEPS) + through(STEPS, m, t)))
                    if m >= 2:
                        act.wait_ge(square_summed.sem, square_summed(l, s * len(SUMS) + replaced(m, t)))
                    nc.scalar.activation(tmp[m % 2][:, TOKENS[t]], x[:, m, TOKENS[t]],
                                         ACT.Square).then_inc(square_ready.sem, 1)

            def root(l, s, t):
                tokens = TOKENS[t]
                act.wait_ge(norm_sum.sem, norm_sum(l, 2 * s + t + 1))
                nc.scalar.activation(ps[RMS_BANK[s % 3][t]][:, tokens], ps[TOTAL_BANK[s % 3][t]][:, tokens],
                                     ACT.Sqrt, bias=eps[:, 0:1], scale=1.0 / D).then_inc(rms_ready.sem, 1)

            def norm(l, s, c0):
                for t in range(2):
                    tokens = TOKENS[t]
                    if s > 0 and t == 0:
                        squares(l, s - 1, STEPS[4:8])
                    if t == 0:
                        for c in range(c0, c0 + (1 if s else 2)):
                            hi(l, c, c % SLOTS)
                    if s > 0 or t == 1:
                        root(l, s, t)
                    if t == 0:
                        if s:
                            hi(l, c0 + 1, (c0 + 1) % SLOTS)
                        act.wait_ge(coef_ready.sem, coef_ready(l, s + 1))
                    for k in range(DK):
                        n = (2 * s + t) * DK + k
                        act.wait_ge(xn_ready.sem, xn_ready(l, n + 1))
                        if k % 2:
                            if k >= 2:
                                act.wait_ge(h_ready.sem, h_ready(l, n - 1))
                            nc.scalar.activation(tmp[3][:, tokens], tmp[1][:, tokens], ACT.Identity,
                                                 bias=mod_shift[:, k:k + 1], scale=mod_gain[:, k:k + 1])
                        nc.scalar.activation(h_hi[:, k, tokens], tmp[k % 2][:, tokens], ACT.Identity,
                                             bias=mod_shift[:, k:k + 1],
                                             scale=mod_gain[:, k:k + 1]).then_inc(h_hi_ready.sem, 1)
                        if t == 0 and k in (2, 5):
                            c = c0 + 2 + k // 3
                            hi(l, c, c % SLOTS)
                        if t == 0 and k in (6, 7):
                            squares(l, s - 1, STEPS[8:10] if k == 6 else STEPS[10:12])

            def ffn(l, f, c0):
                with loop(ENG.Activation, 0, UNITS) as u:
                    for p in range(2):
                        c = c0 + 2 * p
                        hi(l, u * 4 + (c + 4), c % SLOTS)
                        nc.scalar.activation(tmp[p][:], ps[2 * p][:], ACT.Silu).then_inc(bank[2 * p].sem, 1)
                        hi(l, u * 4 + (c + 5), (c + 1) % SLOTS)
                        act.wait_ge(bank[2 * p + 1].sem, bank[2 * p + 1].after(l, f"ffn{f}", u))
                        nc.scalar.activation(tile(act_hi, u * 2 + p), tmp[2 + p][:],
                                             ACT.Copy).then_inc(act_hi_ready.sem, 1)

            def out_product(l, s, c0, n):
                for half in range(2):
                    c = c0 + half * n
                    ahead = n - SLOTS * half
                    loops = ahead // SLOTS if ahead >= 2 * SLOTS else 0
                    if loops:
                        with loop(ENG.Activation, 0, loops) as u:
                            for j in range(SLOTS):
                                hi(l, u * 4 + (c + 4 + j), (c + j) % SLOTS)
                    for j in range(loops * SLOTS, ahead):
                        hi(l, c + 4 + j, (c + j) % SLOTS)
                    if half == 0:
                        squares(l, s, STEPS[:4])
                nc.scalar.activation(table_load[:], eps[:], ACT.Sqrt)

            act.wait_ge(glob_loaded.sem, 32)
            nc.scalar.activation(cond[:], glob[:, G_C:G_C + DK], ACT.Silu).then_inc(cond_ready.sem, 1)
            def begin_ada(g):
                act.wait_ge(cond_ready.sem, 1)
                act.wait_ge(ada_first_loaded[4 * g].sem, 16)
                nc.scalar.activation(ada_total[g][:], ada_now[g][:, 0, :], ACT.Copy,
                                     scale=cond[:, 0:1]).then_inc(ada_first_begun.sem, 1)

            act.wait_ge(x_loaded.sem, 32)
            for m, t in STEPS[:8]:
                if m >= 2:
                    act.wait_ge(square_summed.sem, replaced(m, t))
                nc.scalar.activation(tmp[m % 2][:, TOKENS[t]], x[:, m, TOKENS[t]],
                                     ACT.Square).then_inc(square_ready.sem, 1)
                if m == 1:
                    begin_ada(0)
                if (m, t) == (3, None):
                    act.wait_ge(angles_ready.sem, 2)
                    for i in range(2):
                        nc.scalar.activation(angle[2 + i][:], angle[i][:], ACT.Sin).then_inc(angle_sin.sem, 1)
                    for i in range(2):
                        act.wait_ge(angle_sin.sem, i + 1)
                        act.dma_start(io["rope_scratch"][:, i, :], angle[2 + i][:]).then_inc(rope_stored.sem, 16)
            root(0, 0, 0)
            begin_ada(1)

            with loop(ENG.Activation, 0, LAYERS) as l:
                norm(l, 0, C_FFN1)
                ffn(l, 0, C_FFN1)
                out_product(l, 0, C_FFN1_OUT, UNITS)
                norm(l, 1, C_PROJ)

                def step(j):
                    c = C_PROJ + j + SLOTS
                    hi(l, c, c % SLOTS, tiles_of(c))

                def sc_high(i):
                    act.wait_ge(sc_out_ready.sem, sc_out_ready(l, i + 1))
                    nc.scalar.activation(sc_hi[:, i, :], sc_out[:], ACT.Copy).then_inc(sc_hi_ready.sem, 1)

                for i in range(4):
                    j = 5 * i
                    step(j)
                    step(j + 1)
                    b = (j + 1) % 4
                    nc.scalar.activation(tmp[0][:], ps[b][:], ACT.Sigmoid).then_inc(bank[b].sem, 1)
                    step(j + 2)
                    b = (j + 2) % 4
                    nc.scalar.activation(tmp[1][:], ps[b][:], ACT.Copy).then_inc(bank[b].sem, 1)
                    step(j + 3)
                    if i >= 1:
                        sc_high(i - 1)
                    step(j + 4)
                    b = (j + 4) % 4
                    nc.scalar.activation(tmp[2][:], ps[b][:], ACT.Copy).then_inc(bank[b].sem, 1)

                def qk_root(n):
                    b = NORM_BANK[n]
                    act.wait_ge(qk_norm.sem, qk_norm(l, n + 1))
                    if n >= 1:
                        act.wait_ge(qk_inv.sem, qk_inv(l, n))
                    nc.scalar.activation(tmp[2][:], ps[b][:], ACT.Sqrt, bias=eps[:, 0:1],
                                         scale=1.0 / HD).then_inc(bank[b].sem, 1)

                for j in range(J_K, PROJ_TILES):
                    step(j)
                    n, b = j - J_K, j % 4
                    if n < 5:
                        if n == 1:
                            sc_high(3)
                        if n >= 2:
                            act.wait_ge(qk_norm.sem, qk_norm(l, n - 1))
                        nc.scalar.activation(tmp[n % 2][:], ps[b][:], ACT.Square).then_inc(qk_square.sem, 1)
                        dst = k_pad[:, CHUNK:] if n == 0 else tile(q, n - 1)
                    elif j == J_V:
                        dst = v_pad[:, CHUNK:]
                    else:
                        dst = u_pad[j - J_U][:, UPAD:]
                    nc.scalar.activation(dst, ps[b][:], ACT.Copy).then_inc(bank[b].sem, 1)
                    if 2 <= n < 7:
                        qk_root(n - 2)
                act.wait_ge(v_turned.sem, v_turned(l, 1))
                for b in range(2):
                    nc.scalar.activation(v_tok[:, 4 * b:4 * b + 4, :], ps[4 + b][:].rearrange(
                        "p (c d) -> p c d", c=4), ACT.Copy).then_inc(bank[4 + b].sem, 1)

                def pool_high(g):
                    act.wait_ge(pool_out.sem, pool_out(l, g + 1))
                    nc.scalar.activation(pool_hi[:, g, :], pair[g % 2][:], ACT.Copy).then_inc(pool_hi_ready.sem, 1)

                def pool_branch(half, beside):
                    c = C_POOL + 5 * half
                    for i in range(4):
                        m = 4 * half + i
                        hi(l, c + 4 + i, (c + i) % SLOTS, tiles_of(c + 4 + i))
                        nc.scalar.activation(tile(merged, m), ps[i][:], ACT.Sigmoid,
                                             bias=par_col("b_gate", DK + m)).then_inc(bank[i].sem, 1)
                        beside(i)

                def pool_fill(half):
                    c = C_POOL + 5 * half + 4
                    hi(l, c + 4, c % SLOTS, tiles_of(c + 4))

                act.wait_ge(sc_ready.sem, sc_ready(l, 4))
                def beside_second(i):
                    if i == 1:
                        for t in range(4):
                            act.wait_ge(xc_ready.sem, xc_ready(l, t + 1))
                            if t >= 2:
                                act.wait_ge(xc_summed.sem, xc_summed(l, t - 1))
                            nc.scalar.activation(xc_sq[t % 2][:], conv_out[t][:], ACT.Square).then_inc(xc_square.sem, 1)
                    elif i == 2:
                        act.wait_ge(ln_var.sem, ln_var(l, 1))
                        nc.scalar.activation(xc_sq[0][:], ps[4][:], ACT.Sqrt, bias=eps[:, 0:1],
                                             scale=1.0 / (4 * P)).then_inc(ln_rms.sem, 1)

                def give_q(p):
                    nc.scalar.activation(q_now[:], tile(q, p), ACT.Copy).then_inc(q_now_ready.sem, 1)

                pool_branch(0, pool_high)
                pool_fill(0)
                pool_branch(1, beside_second)
                give_q(0)
                pool_fill(1)
                for i in range(4):
                    act.wait_ge(ln_y.sem, ln_y(l, i + 1))
                    nc.scalar.activation(conv_hi[:, i, :], conv_out[i][:], ACT.Silu, bias=par_col("ln_b", i),
                                         scale=par_col("ln_g", i))
                    nc.scalar.activation(conv_out[i][:], conv_out[i][:], ACT.Silu, bias=par_col("ln_b", i),
                                         scale=par_col("ln_g", i)).then_inc(conv_silu.sem, 1)
                act.wait_ge(bank[7].sem, bank[7].after(l, "pool1"))

                def pair_step(l, p, name, c0, which, scores=False, split_merged=False, last=False):
                    for e in range(2):
                        c = c0 + 2 * e
                        hi(l, p * 4 + (c + 4), c % SLOTS)
                        act.wait_ge(bank[2 * e + 1].sem, bank[2 * e + 1].before(l, name, p))
                        nc.scalar.activation(tmp[e][:], ps[2 * e][:], ACT.Sigmoid,
                                             bias=par_col("b_gate", p * 2 + (which * DK + e))
                                             ).then_inc(bank[2 * e].sem, 1)
                        hi(l, p * 4 + (c + 5), (c + 1) % SLOTS, 8 if last else 4)
                        if scores and e == 0:
                            act.wait_ge(neg_max.sem, neg_max(l, p + 1))
                            for ch in range(NCH):
                                b = 4 + ch // 4
                                first = CHUNK if ch == 0 else 0
                                ins = nc.scalar.activation(
                                    probs[:, ch, first:], ps[b][:, (ch % 4) * P + first:(ch % 4 + 1) * P], ACT.Exp,
                                    bias=soft[:, 1, ch:ch + 1], scale=HD ** -0.5, accum_out=soft[:, 2, ch:ch + 1])
                                if ch % 4 == 3:
                                    ins.then_inc(bank[b].sem, 1)
                            nc.scalar.activation(soft[:, 3, :], soft[:, 1, :], ACT.Exp,
                                                 bias=par_col("sink", p)).then_inc(exp_ready.sem, 1)
                        if split_merged:
                            act.wait_ge(merged_ready.sem, merged_ready(l, p * 2 + (2 * DK + e + 1)))
                            nc.scalar.activation(tile(mixed_hi, p * 2 + e), tile(merged, p * 2 + e),
                                                 ACT.Copy).then_inc(mixed_hi_ready.sem, 1)
                    if scores:
                        act.wait_ge(probs_turned.sem, probs_turned(l, p + 1))
                        for b in range(2):
                            nc.scalar.activation(probs_t[:, 4 * b:4 * b + 4, :, bass.ds(p, 1), :],
                                                 ps[6 + b][:].rearrange("p (c g t) -> p c g t", c=4, g=2),
                                                 ACT.Copy).then_inc(bank[6 + b].sem, 1)

                pair_step(l, 0, "sc", C_SC, 3, scores=True)
                with loop(ENG.Activation, 1, 4) as p:
                    give_q(p)
                    pair_step(l, p, "sc", C_SC, 3, scores=True)
                act.wait_ge(pv_ready.sem, pv_ready(l, 1))
                for b in range(4):
                    nc.scalar.activation(o_hi[:, :, P * b:P * b + P].rearrange("p i (c t) -> p c i t", c=2),
                                         ps[4 + b][:].rearrange("p (c i t) -> p c i t", c=2, i=QT),
                                         ACT.Copy).then_inc(o_hi_ready.sem, 1)
                with loop(ENG.Activation, 0, 4) as p:
                    pair_step(l, p, "conv", C_CONV, 2)
                with loop(ENG.Activation, 0, 3) as p:
                    pair_step(l, p, "attn", C_ATTN, 0, split_merged=True)
                pair_step(l, 3, "attn", C_ATTN, 0, split_merged=True, last=True)
                out_product(l, 1, C_WO, DK // 2)
                norm(l, 2, C_FFN2)
                ffn(l, 1, C_FFN2)
                out_product(l, 2, C_FFN2_OUT, UNITS)
                squares(l, 2, STEPS[4:8])
                root(l, 3, 0)

        @block.vector
        def _(dve):
            V = nc.vector
            links = [0]

            def link(ins):
                links[0] += 1
                ins.then_inc(setup_step.sem, 1)
                dve.wait_ge(setup_step.sem, links[0])

            dve.sem_inc(ada_free.sem, 2)
            dve.sem_inc(x_updated.sem, len(STEPS))
            dve.sem_inc(merged_ready.sem, 1)
            link(V.memset(eps[:], EPS))
            dve.wait_ge(glob_loaded.sem, 32)
            a, turns = angle[0], angle[1]
            link(V.tensor_copy(a[:], angle_i[:]))
            link(V.tensor_scalar(a[:], a[:], glob[:, G_FREQ:G_FREQ + 1], None, ALU.mult))
            for unit in (4096.0, 1.0):
                link(V.tensor_scalar(turns[:], a[:], 1.0 / (TWO_PI * unit), ROUND, ALU.mult, ALU.add))
                link(V.tensor_scalar(turns[:], turns[:], ROUND, None, ALU.subtract))
                for part in TURN:
                    link(V.scalar_tensor_tensor(a[:], turns[:], -part * unit, a[:], ALU.mult, ALU.add))
            V.tensor_scalar(angle[1][:], a[:], 3.1415925, -3.1415925, ALU.min, ALU.max).then_inc(angles_ready.sem, 1)
            dve.wait_ge(angles_ready.sem, 1)
            link(V.scalar_tensor_tensor(a[:], angle[1][:], -1.0, angle[1][:], ALU.mult, ALU.max))
            V.tensor_scalar(a[:], a[:], -1.0, TWO_PI / 4, ALU.mult, ALU.add).then_inc(angles_ready.sem, 1)
            for g in range(ADA_FIRST):
                for k in range(1, DK):
                    dve.wait_ge(ada_first_loaded[g * 4 + k // 2].sem, 16)
                    if k == 1:
                        dve.wait_ge(ada_first_begun.sem, g + 1)
                    link(V.scalar_tensor_tensor(ada_total[g][:], ada_now[g][:, k, :], cond[:, k:k + 1],
                                                ada_total[g][:], ALU.mult, ALU.add))
                V.sem_inc(ada_first_summed.sem, 1)
            dve.wait_ge(rope_stored.sem, 32)

            def add_square(l, s, m, t):
                dve.wait_ge(square_ready.sem, square_ready(l, s * len(STEPS) + through(STEPS, m, t)))
                if m >= 2:
                    dve.wait_ge(square_summed.sem, square_summed(l, s * len(SUMS) + through(SUMS, m, t) - 1))
                V.tensor_tensor(tmp[2][:, TOKENS[t]], tmp[0 if m == 1 else 2][:, TOKENS[t]],
                                tmp[m % 2][:, TOKENS[t]], ALU.add).then_inc(square_summed.sem, 1)

            def update(l, s, m, t):
                b = m + 4 if m < 4 else m if s != 1 else m - 4
                if s != 1 and m >= 4:
                    dve.wait_ge(x_begun.sem, x_begun(l, s // 2 * 4 + m - 3))
                V.scalar_tensor_tensor(x[:, m, TOKENS[t]], ps[b][:, TOKENS[t]], mod_gate[:, m:m + 1],
                                       x[:, m, TOKENS[t]], ALU.mult, ALU.add).then_inc(x_updated.sem, 1)

            def begin_update(l, s, c):
                V.tensor_scalar(mod_gate[:], mod_cols(l, 3 * s + 2), 1.0 if s == 1 else 0.5, None,
                                ALU.mult).then_inc(gate_coef.sem, 1)
                dve.wait_ge(gate_coef.sem, gate_coef(l, s + 1))
                for m in range(4):
                    if m < 3:
                        dve.wait_ge(out_tile.sem, out_tile(l, s * OUT_TILES + m + 1))
                    else:
                        dve.wait_ge(used.sem, used(l, c + 1))
                    update(l, s, m, None)
                    if m >= 2:
                        add_square(l, s, m - 1, None)
                add_square(l, s, 3, None)
                if s != 1:
                    dve.wait_ge(used.sem, used(l, c + 1 + UNITS - SLOTS))
                    for m in range(4, DK):
                        V.scalar_tensor_tensor(x[:, m, :], ps[m - 4][:], mod_gate[:, m:m + 1], x[:, m, :],
                                               ALU.mult, ALU.add).then_inc(x_begun.sem, 1)

            def end_update(l, s, t, c, tiles, adds):
                for m in tiles:
                    if (m, t) == STEPS[-1]:
                        dve.wait_ge(used.sem, used(l, c + 1))
                    else:
                        dve.wait_ge(out_tile.sem, out_tile(l, s * OUT_TILES + through(STEPS, m, t) - 1))
                    update(l, s, m, t)
                for m in adds:
                    add_square(l, s, m, t)

            def invert(l, s, t):
                inv = ps[RMS_BANK[s % 3][t]][:, TOKENS[t]]
                dve.wait_ge(rms_ready.sem, rms_ready(l, 2 * s + t + 1))
                V.reciprocal(inv, inv).then_inc(inv_rms.sem, 1)

            def norm(l, s, c=None):
                dve.wait_ge(mods_done.sem, mods_done(l, HALVES if s else 0))
                dve.wait_ge(par_loaded.sem, par_loaded(l, 16))
                V.scalar_tensor_tensor(mod_gain[:], mod_cols(l, 3 * s + 1), 1.0,
                                       par[:, PAR["gain"] + s * DK:PAR["gain"] + s * DK + DK], ALU.add, ALU.mult)
                V.tensor_copy(mod_shift[:], mod_cols(l, 3 * s)).then_inc(coef_ready.sem, 1)
                dve.wait_ge(coef_ready.sem, coef_ready(l, s + 1))
                for t in range(2):
                    tokens = TOKENS[t]
                    if s > 0 and t == 0:
                        end_update(l, s - 1, t, c, (4, 5), (4, 5))
                        end_update(l, s - 1, t, c, (6, 7), (6, 7))
                    if s > 0 or t == 1:
                        invert(l, s, t)
                    inv = ps[RMS_BANK[s][t]][:, tokens]
                    dve.wait_ge(inv_rms.sem, inv_rms(l, 2 * s + t + 1))
                    for k in range(DK + 1):
                        if s > 0 and t == 0 and k in (4, 6):
                            end_update(l, s - 1, 1, c, (k, k + 1), ())
                        n = (2 * s + t) * DK + k
                        if k < DK:
                            if k >= 2:
                                dve.wait_ge(h_hi_ready.sem, h_hi_ready(l, n - 1))
                            V.tensor_tensor(tmp[k % 2][:, tokens], x[:, k, tokens], inv,
                                            ALU.mult).then_inc(xn_ready.sem, 1)
                        if k < DK and k % 2 == 0:
                            dve.wait_ge(xn_ready.sem, xn_ready(l, n + 1))
                            if k >= 2:
                                dve.wait_ge(h_ready.sem, h_ready(l, n - 1))
                            V.tensor_scalar(tmp[2][:, tokens], tmp[0][:, tokens], mod_gain[:, k:k + 1],
                                            mod_shift[:, k:k + 1], ALU.mult, ALU.add).then_inc(h_whole.sem, 1)
                        if k >= 1:
                            dve.wait_ge(h_hi_ready.sem, h_hi_ready(l, n))
                            if k % 2:
                                dve.wait_ge(h_whole.sem, h_whole(l, (n + 1) // 2))
                            V.tensor_tensor(h_lo[:, k - 1, tokens], tmp[2 + (k - 1) % 2][:, tokens],
                                            h_hi[:, k - 1, tokens].bitcast(F32), ALU.subtract).then_inc(h_ready.sem, 1)
                    if t == 0:
                        end_update(l, s - 1, 1, c, (), (4, 5, 6, 7))

            def ffn(l, f, c0):
                def product(u, p):
                    dve.wait_ge(used.sem, used(l, u * 4 + (c0 + 2 * p + 2)))
                    dve.wait_ge(bank[2 * p].sem, bank[2 * p].after(l, f"ffn{f}", u))
                    V.tensor_tensor(tmp[2 + p][:], tmp[p][:], ps[2 * p + 1][:],
                                    ALU.mult).then_inc(bank[2 * p + 1].sem, 1)

                def low(u, p):
                    n = u * 2 + p
                    dve.wait_ge(act_hi_ready.sem, act_hi_ready(l, n + (f * FK + 1)))
                    V.tensor_tensor(tile(act_lo, n), tmp[2 + p][:], tile(act_hi, n).bitcast(F32),
                                    ALU.subtract).then_inc(act_ready.sem, 1)

                def store_mods(h):
                    dve.wait_ge(ada_sum.sem, ada_sum(l, h + 1))
                    col = l * (HALVES * 4) + (h * 4 + ADA_FIRST * DK)
                    V.tensor_tensor(mods[:, bass.ds(col, 4)], ps[7][:, 0:4], glob[:, bass.ds(col, 4)],
                                    ALU.add).then_inc(mods_done.sem, 1)

                def ada(h):
                    for i in range(PIECES):
                        piece = h * PIECES + i
                        b = i % 2
                        dve.wait_ge(ada_loaded[b].sem, ada_loaded[b](l, h * (16 * PIECES // 2) + 16 * (i // 2 + 1)))
                        if i == 0:
                            V.tensor_scalar(ada_acc[:], ada_buf[b][:, 0, :], cond[:, 0:1], None,
                                            ALU.mult).then_inc(ada_step.sem, 1)
                        else:
                            dve.wait_ge(ada_free.sem, ada_free(l, piece))
                            V.scalar_tensor_tensor(ada_acc[:], ada_buf[b][:, 0, :], cond[:, 2 * i:2 * i + 1],
                                                   ada_acc[:], ALU.mult, ALU.add).then_inc(ada_step.sem, 1)
                        dve.wait_ge(ada_step.sem, ada_step(l, piece + 1))
                        V.scalar_tensor_tensor(ada_acc[:], ada_buf[b][:, 1, :], cond[:, 2 * i + 1:2 * i + 2],
                                               ada_acc[:], ALU.mult, ALU.add).then_inc(ada_free.sem, 1)

                def unit(u, store, more):
                    for p in range(2):
                        product(u, p)
                        if store[p]:
                            store_mods(u * 2 + (p - 1))
                        if more[p]:
                            ada(u * 2 + p)
                        low(u, p)

                if f == 0:
                    unit(0, (False, True), (True, True))
                    with loop(ENG.DVE, 1, ADA_STEP) as u:
                        unit(u, (True, True), (True, True))
                    unit(ADA_STEP, (True, False), (False, False))
                    unit(ADA_STEP + 1, (False, False), (False, False))
                else:
                    with loop(ENG.DVE, 0, UNITS) as u:
                        unit(u, (False, False), (False, False))

            invert(0, 0, 0)
            dve.wait_ge(ada_first_ready.sem, 1)
            n = ADA_FIRST * DK
            V.tensor_tensor(mods[:, 0:n], ps[7][:, 0:n], glob[:, G_ADA_B:G_ADA_B + n],
                            ALU.add).then_inc(mods_done.sem, 1)
            with loop(ENG.DVE, 0, LAYERS) as l:
                norm(l, 0)
                ffn(l, 0, C_FFN1)
                begin_update(l, 0, C_FFN1_OUT + UNITS - 1)
                norm(l, 1, C_PROJ - 1)

                for pad in [z[:, 0:TAPS - 1] for z in z_pad] + [s_pad[:, 0:SC_TAPS - 1], v_pad[:, 0:CHUNK]] \
                        + [probs[:, 0, 0:CHUNK]] + [u[:, 0:UPAD] for u in u_pad]:
                    V.memset(pad, 0.0)
                V.tensor_scalar(neg_sink[:], par[:, PAR["sink"]:PAR["sink"] + QT], -1.0, None,
                                ALU.mult).then_inc(pads_ready.sem, 1)
                dve.wait_ge(pads_ready.sem, pads_ready(l, 1))

                def proj_bank(j):
                    phase = ("proj", j // 4) if j < 28 else ("proj_tail", 0)
                    return j % 4, phase

                def read_by_scalar(j):
                    b, (phase, time) = proj_bank(j)
                    dve.wait_ge(bank[b].sem, bank[b].after(l, phase, time))

                def sc_low(i):
                    dve.wait_ge(sc_hi_ready.sem, sc_hi_ready(l, i + 1))
                    V.tensor_tensor(sc_lo[:, i, :], sc_out[:], sc_hi[:, i, :].bitcast(F32),
                                    ALU.subtract).then_inc(sc_ready.sem, 1)

                for i in range(4):
                    j = 5 * i
                    z, acc = z_pad[i % 2], (conv_out[i], odd_taps)
                    read_by_scalar(j + 1)
                    V.tensor_tensor(z[:, TAPS - 1:], ps[j % 4][:], tmp[0][:], ALU.mult).then_inc(bank[j % 4].sem, 1)
                    read_by_scalar(j)
                    for t in range(TAPS):
                        src, w = z[:, t:t + T], par_col("conv_w", i * TAPS + t)
                        if t >= 2:
                            dve.wait_ge(conv_tap.sem, conv_tap(l, i * (TAPS + 1) + t - 1))
                            ins = V.scalar_tensor_tensor(acc[t % 2][:], src, w, acc[t % 2][:], ALU.mult, ALU.add)
                        elif t == 1:
                            if i >= 1:
                                dve.wait_ge(conv_tap.sem, conv_tap(l, i * (TAPS + 1)))
                            ins = V.tensor_scalar(acc[1][:], src, w, None, ALU.mult)
                        else:
                            ins = V.tensor_scalar(acc[0][:], src, w, par_col("conv_b", i), ALU.mult, ALU.add)
                        ins.then_inc(conv_tap.sem, 1)
                        if t == 12:
                            dve.wait_ge(used.sem, used(l, C_PROJ + j + 4))
                            read_by_scalar(j + 2)
                            b = (j + 3) % 4
                            V.tensor_tensor(s_pad[:, SC_TAPS - 1:], ps[b][:], tmp[1][:],
                                            ALU.mult).then_inc(bank[b].sem, 1)
                    dve.wait_ge(conv_tap.sem, conv_tap(l, i * (TAPS + 1) + TAPS))
                    V.tensor_tensor(acc[0][:], acc[0][:], acc[1][:], ALU.add).then_inc(conv_tap.sem, 1)
                    if i >= 1:
                        sc_low(i - 1)
                    read_by_scalar(j + 3)
                    for t in range(SC_TAPS):
                        src, w = s_pad[:, t:t + T], par_col("sc_w", i * SC_TAPS + t)
                        if t == 0:
                            if i >= 1:
                                dve.wait_ge(sc_out_ready.sem, sc_out_ready(l, i))
                            V.tensor_scalar(s_conv[:], src, w, None, ALU.mult).then_inc(sc_tap.sem, 1)
                        else:
                            V.scalar_tensor_tensor(s_conv[:], src, w, s_conv[:], ALU.mult,
                                                   ALU.add).then_inc(sc_tap.sem, 1)
                        dve.wait_ge(sc_tap.sem, sc_tap(l, i * SC_TAPS + t + 1))
                    read_by_scalar(j + 4)
                    if i >= 1:
                        dve.wait_ge(sc_ready.sem, sc_ready(l, i))
                    V.tensor_tensor(sc_out[:], s_conv[:], tmp[2][:], ALU.mult).then_inc(sc_out_ready.sem, 1)

                def rotate(n):
                    raw_qk = k_pad[:, CHUNK:] if n == 0 else tile(q, n - 1)
                    if n >= 1:
                        dve.wait_ge(qk_ready.sem, qk_ready(l, n))
                    V.tensor_tensor(pair[0][:], raw_qk, rope_tab[:, 0, :], ALU.mult).then_inc(rope_part.sem, 1)
                    dve.wait_ge(qk_turned.sem, qk_turned(l, n + 1))
                    b = ROPE_BANK[n]
                    V.tensor_tensor(pair[1][:], ps[b][:], rope_tab[:, 1, :], ALU.mult).then_inc(bank[b].sem, 1)
                    dve.wait_ge(rope_part.sem, rope_part(l, n + 1))
                    dve.wait_ge(bank[b].sem, bank[b].after(l, f"rope{n}"))
                    V.tensor_tensor(raw_qk, pair[0][:], pair[1][:], ALU.add).then_inc(qk_ready.sem, 1)

                for n in range(6):
                    if n < 5:
                        raw_qk = k_pad[:, CHUNK:] if n == 0 else tile(q, n - 1)
                        b = NORM_BANK[n]
                        dve.wait_ge(bank[b].sem, bank[b].after(l, f"norm{n}"))
                        if n >= 1:
                            dve.wait_ge(qk_normed.sem, qk_normed(l, n))
                        V.reciprocal(tmp[3][:], tmp[2][:]).then_inc(qk_inv.sem, 1)
                        dve.wait_ge(qk_inv.sem, qk_inv(l, n + 1))
                        V.scalar_tensor_tensor(raw_qk, raw_qk, par_col("q_gain" if n else "k_gain"), tmp[3][:],
                                               ALU.mult, ALU.mult).then_inc(qk_normed.sem, 1)
                    if n == 0:
                        sc_low(3)
                        dve.wait_ge(rope_loaded.sem, rope_loaded(l, 16))
                    else:
                        dve.wait_ge(qk_normed.sem, qk_normed(l, n))
                        rotate(n - 1)
                    if n == 1:
                        dve.wait_ge(qk_ready.sem, qk_ready(l, 1))
                        V.tensor_copy(k_pad[:, 0:CHUNK], k_pad[:, CHUNK:2 * CHUNK]).then_inc(k_first.sem, 1)

                def pool_low(g):
                    dve.wait_ge(pool_hi_ready.sem, pool_hi_ready(l, g + 1))
                    V.tensor_tensor(pool_lo[:, g, :], pair[g % 2][:], pool_hi[:, g, :].bitcast(F32),
                                    ALU.subtract).then_inc(pool_ready.sem, 1)

                steps = 0
                for g, w in enumerate(WINDOWS):
                    read_by_scalar(J_U + g)
                    if g >= 1:
                        dve.wait_ge(pool_out.sem, pool_out(l, g))
                    src, start = u_pad[g], 0
                    for st in range(g + 1):
                        start += 2 ** st
                        V.tensor_tensor(window[st % 2][:, start:], src[:, start:], src[:, start - 2 ** st:UPAD + T - 2 ** st],
                                        ALU.add).then_inc(window_step.sem, 1)
                        steps += 1
                        dve.wait_ge(window_step.sem, window_step(l, steps))
                        src = window[st % 2]
                    col = G_COUNT + g * UPAD
                    V.tensor_tensor(src[:, UPAD:2 * UPAD], src[:, UPAD:2 * UPAD], glob[:, col:col + UPAD],
                                    ALU.mult).then_inc(window_step.sem, 1)
                    steps += 1
                    dve.wait_ge(window_step.sem, window_step(l, steps))
                    if g >= 2:
                        dve.wait_ge(pool_ready.sem, pool_ready(l, g - 1))
                    else:
                        dve.wait_ge(qk_ready.sem, qk_ready(l, 5))
                    V.scalar_tensor_tensor(pair[g % 2][:], src[:, UPAD:], 1.0 / w, u_pad[g][:, UPAD:], ALU.mult,
                                           ALU.subtract).then_inc(pool_out.sem, 1)
                    if g >= 1:
                        pool_low(g - 1)
                pool_low(3)

                dve.wait_ge(pool_ready.sem, pool_ready(l, 4))
                for i in range(1, 4):
                    if i >= 2:
                        dve.wait_ge(ln_sum.sem, ln_sum(l, i - 1))
                    V.tensor_tensor(pair[1][:], conv_out[0][:] if i == 1 else pair[1][:], conv_out[i][:],
                                    ALU.add).then_inc(ln_sum.sem, 1)

                def pool_merge(half):
                    dve.wait_ge(used.sem, used(l, C_POOL + 5 * half + 5))
                    for i in range(4):
                        m = 4 * half + i
                        dve.wait_ge(bank[i].sem, bank[i].after(l, f"pool{half}"))
                        V.scalar_tensor_tensor(tile(merged, m), ps[4 + i][:], par_col("pool_scale", m),
                                               tile(merged, m), ALU.mult, ALU.mult).then_inc(bank[4 + i].sem, 1)

                pool_merge(0)
                dve.wait_ge(ln_mean.sem, ln_mean(l, 1))
                for i in range(4):
                    V.scalar_tensor_tensor(conv_out[i][:], ps[3][:], -1.0 / (4 * P), conv_out[i][:], ALU.mult,
                                           ALU.add).then_inc(xc_ready.sem, 1)
                for i in range(4):
                    dve.wait_ge(xc_square.sem, xc_square(l, i + 1))
                    if i == 0:
                        V.tensor_copy(pair[1][:], xc_sq[0][:]).then_inc(xc_summed.sem, 1)
                    else:
                        dve.wait_ge(xc_summed.sem, xc_summed(l, i))
                        V.tensor_tensor(pair[1][:], pair[1][:], xc_sq[i % 2][:], ALU.add).then_inc(xc_summed.sem, 1)
                dve.wait_ge(ln_rms.sem, ln_rms(l, 1))
                V.reciprocal(xc_sq[1][:], xc_sq[0][:]).then_inc(ln_inv.sem, 1)
                dve.wait_ge(ln_inv.sem, ln_inv(l, 1))
                for i in range(4):
                    V.tensor_tensor(conv_out[i][:], conv_out[i][:], xc_sq[1][:], ALU.mult).then_inc(ln_y.sem, 1)
                pool_merge(1)
                for i in range(4):
                    dve.wait_ge(conv_silu.sem, conv_silu(l, i + 1))
                    V.tensor_tensor(conv_lo[:, i, :], conv_out[i][:], conv_hi[:, i, :].bitcast(F32),
                                    ALU.subtract).then_inc(conv_ready.sem, 1)

                def merge(p, e, name, c0, n0):
                    dve.wait_ge(used.sem, used(l, p * 4 + (c0 + 2 * e + 2)))
                    dve.wait_ge(bank[2 * e].sem, bank[2 * e].after(l, name, p))
                    y = bank[2 * e + 1]
                    dve.wait_ge(merged_ready.sem, merged_ready(l, p * 2 + (n0 + e)))
                    V.tensor_tensor(tmp[2][:], tmp[e][:], ps[2 * e + 1][:], ALU.mult).then_inc(y.sem, 1)
                    dve.wait_ge(y.sem, y.after(l, name, p))
                    V.tensor_tensor(tile(merged, p * 2 + e), tile(merged, p * 2 + e), tmp[2][:],
                                    ALU.add).then_inc(merged_ready.sem, 1)

                with loop(ENG.DVE, 0, 4) as p:
                    dve.wait_ge(scores_ready.sem, scores_ready(l, p + 1))
                    for b in range(2):
                        ins = V.tensor_reduce(soft[:, 0, 4 * b:4 * b + 4],
                                              ps[4 + b][:].rearrange("p (c k) -> p c k", c=4), AX.X, ALU.max)
                    ins.then_inc(max_found.sem, 1)
                    dve.wait_ge(max_found.sem, max_found(l, p + 1))
                    V.tensor_scalar(soft[:, 1, :], soft[:, 0, :], -(HD ** -0.5), neg_sink[:, bass.ds(p, 1)],
                                    ALU.mult, ALU.min).then_inc(neg_max.sem, 1)
                    merge(p, 0, "sc", C_SC, 0)
                    dve.wait_ge(exp_ready.sem, exp_ready(l, p + 1))
                    V.tensor_tensor(soft[:, 4, :], soft[:, 2, :], soft[:, 3, :], ALU.add).then_inc(total_ready.sem, 1)
                    dve.wait_ge(total_ready.sem, total_ready(l, p * 2 + 1))
                    V.reciprocal(soft[:, 4, :], soft[:, 4, :]).then_inc(total_ready.sem, 1)
                    dve.wait_ge(total_ready.sem, total_ready(l, p * 2 + 2))
                    V.tensor_tensor(probs[:], probs[:], soft[:, 4, :].unsqueeze(2).broadcast_to((P, NCH, P)),
                                    ALU.mult).then_inc(probs_ready.sem, 1)
                    merge(p, 1, "sc", C_SC, 0)
                for b in range(4):
                    dve.wait_ge(o_hi_ready.sem, o_hi_ready(l, b + 1))
                    tokens = slice(P * b, P * b + P)
                    V.tensor_tensor(o_lo[:, :, tokens].rearrange("p i (c t) -> p c i t", c=2),
                                    ps[4 + b][:].rearrange("p (c i t) -> p c i t", c=2, i=QT),
                                    o_hi[:, :, tokens].bitcast(F32).rearrange("p i (c t) -> p c i t", c=2),
                                    ALU.subtract).then_inc(bank[4 + b].sem, 1)
                with loop(ENG.DVE, 0, 4) as p:
                    for e in range(2):
                        merge(p, e, "conv", C_CONV, DK)
                with loop(ENG.DVE, 0, 4) as p:
                    for e in range(2):
                        merge(p, e, "attn", C_ATTN, 2 * DK)
                        dve.wait_ge(mixed_hi_ready.sem, mixed_hi_ready(l, p * 2 + (e + 1)))
                        V.tensor_tensor(tile(mixed_lo, p * 2 + e), tile(merged, p * 2 + e),
                                        tile(mixed_hi, p * 2 + e).bitcast(F32), ALU.subtract).then_inc(mixed_ready.sem, 1)
                begin_update(l, 1, C_WO + DK // 2 - 1)
                norm(l, 2, C_FFN2 - 1)
                ffn(l, 1, C_FFN2)
                begin_update(l, 2, C_FFN2_OUT + UNITS - 1)
                end_update(l, 2, 0, CHUNKS - 1, (4, 5), (4, 5))
                end_update(l, 2, 0, CHUNKS - 1, (6, 7), (6, 7))
                invert(l, 3, 0)
                end_update(l, 2, 1, CHUNKS - 1, range(4, DK), ())

        @block.tensor
        def _(pe):
            pe.sem_inc(used.sem, SLOTS)
            for b in range(8):
                pe.sem_inc(bank[b].sem, 1)

            def product(out, slot, i, rhs_hi, rhs_lo, start, stop):
                nc.tensor.matmul(out, whi[slot][:, i, :], rhs_hi, start=start, stop=False)
                nc.tensor.matmul(out, whi[slot][:, i, :], rhs_lo, start=False, stop=False)
                return nc.tensor.matmul(out, wlo[slot][:, i, :], rhs_hi, start=False, stop=stop)

            def carry_waits():
                pe.sem_inc(waits_carried.sem, 1)

            def norm_total(l, s, t):
                pe.wait_ge(square_summed.sem, square_summed(l, (s - 1) * len(SUMS) + through(SUMS, 7, t)))
                nc.tensor.matmul(ps[TOTAL_BANK[s % 3][t]][:, TOKENS[t]], ones, tmp[2][:, TOKENS[t]], start=True,
                                 stop=True).then_inc(norm_sum.sem, 1)

            def first_four(l, s, c0, phase):
                for t in range(2):
                    tokens = TOKENS[t]
                    for first in (0, 2):
                        if t == 0:
                            for j in (first, first + 1):
                                pe.wait_ge(bank[j].sem, bank[j].before(l, phase))
                            if s == 2:
                                pe.wait_ge(x_updated.sem, x_updated(l, (s - 1) * len(STEPS) + through(STEPS, 5 + first, 1)))
                            pe.wait_ge(split.sem, split(l, c0 + first + 2))
                        for k in range(DK):
                            if first == 0:
                                pe.wait_ge(h_ready.sem, h_ready(l, (2 * s + t) * DK + k + 1))
                            if t == 0 and (first, k) == (2, 2):
                                norm_total(l, s, 1)
                            for j in (first, first + 1):
                                mm = product(ps[j][:, tokens], (c0 + j) % SLOTS, k, h_hi[:, k, tokens],
                                             h_lo[:, k, tokens], k == 0, k == DK - 1)
                                if t == 1 and k == DK - 1:
                                    mm.then_inc(used.sem, 1)

            def ffn(l, f, s, c0):
                def unit(u, sums=(False, False)):
                    for p in range(2):
                        c = c0 + 2 * p
                        pe.wait_ge(bank[2 * p].sem, bank[2 * p].before(l, f"ffn{f}", u))
                        pe.wait_ge(bank[2 * p + 1].sem, bank[2 * p + 1].before(l, f"ffn{f}", u))
                        pe.wait_ge(split.sem, split(l, u * 4 + (c + 2)))
                        for k in range(DK):
                            if k == 6 and sums[p]:
                                ada_sums(u * 2 + (p - 2))
                            for side in range(2):
                                mm = product(ps[2 * p + side][:], (c + side) % SLOTS, k, h_hi[:, k, :], h_lo[:, k, :],
                                             k == 0, k == DK - 1)
                                if k == DK - 1:
                                    mm.then_inc(used.sem, 1)

                def ada_sums(h):
                    pe.wait_ge(ada_free.sem, ada_free(l, (h + 1) * PIECES))
                    for m in range(4):
                        mm = nc.tensor.matmul(ps[7][:, m:m + 1], ada_acc[:, P * m:P * m + P], ones[:, 0:1],
                                              start=True, stop=True)
                    mm.then_inc(ada_sum.sem, 1)

                first_four(l, s, c0, f"ffn{f}")
                if f == 0:
                    with loop(ENG.PE, 1, ADA_STEP + 1) as u:
                        unit(u, sums=(True, True))
                    unit(ADA_STEP + 1)
                else:
                    with loop(ENG.PE, 1, UNITS) as u:
                        unit(u)

            def out_product(l, s, c0, n, ready, ready_at, rhs_hi, rhs_lo):
                whole = n - SLOTS

                def chunk(k, c, c_static, banks, t=None, tiles=range(4), first=False, last=False, begun=False,
                          total=False):
                    if t != 1 and tiles[0] == 0:
                        pe.wait_ge(split.sem, split(l, c + 1))
                    order = [(kk, i) for i in tiles for kk in range(2)] if last or begun else \
                        [(kk, i) for kk in range(2) for i in tiles]
                    tokens = TOKENS[t]
                    for kk, i in order:
                        if total and (kk, i) == (1, 0):
                            norm_total(l, s + 1, 0)
                        if begun and kk == 0 and i % 2 == 0:
                            pe.wait_ge(x_updated.sem, x_updated(l, s * len(STEPS) + through(STEPS, 5 + i, 0)))
                        here = bass.ds((k + kk) * T + tokens.start, tokens.stop - tokens.start)
                        mm = product(ps[banks + i][:, tokens], c_static % SLOTS, 4 * kk + i, rhs_hi[:, here],
                                     rhs_lo[:, here], first and kk == 0, last and kk == 1)
                        if last and kk == 1 and (i < 3 or t == 0) and (t, banks) != (None, 0):
                            mm.then_inc(out_tile.sem, 1)
                    if t != 0:
                        mm.then_inc(used.sem, 1)

                for b in range(4, 8):
                    pe.wait_ge(bank[b].sem, bank[b].before(l, f"out{s}"))

                def first_tiles(k, c, c_static, first=False, last=False):
                    pe.wait_ge(ready.sem, ready(l, ready_at + k + 2))
                    chunk(k, c, c_static, 4, first=first, last=last)

                first_tiles(0, c0, c0, first=True)
                loops = (n - 2) // SLOTS if n > 2 * SLOTS else 0
                if loops:
                    with loop(ENG.PE, 0, loops) as u:
                        for j in range(SLOTS):
                            first_tiles(u * 8 + (2 + 2 * j), u * 4 + (c0 + 1 + j), c0 + 1 + j)
                for j in range(1 + SLOTS * loops, n):
                    first_tiles(2 * j, c0 + j, c0 + j, last=j == n - 1)

                for b in range(4):
                    pe.wait_ge(bank[b].sem, bank[b].before(l, f"out{s}"))
                c = c0 + n
                for j in range(whole):
                    chunk(2 * j, c + j, c + j, 0, first=j == 0, last=j == whole - 1)
                banks = 4 if whole else 0
                if whole:
                    pe.wait_ge(x_updated.sem, x_updated(l, s * len(STEPS) + through(STEPS, 3, None)))
                for tiles in (range(0, 2), range(2, 4)):
                    for j in range(whole, n):
                        chunk(2 * j, c + j, c + j, banks, 0, tiles, first=j == whole, last=j == n - 1)
                for j in range(whole, n):
                    chunk(2 * j, c + j, c + j, banks, 1, first=j == whole, last=j == n - 1, begun=j == whole,
                          total=j == whole + 1)

            pe.wait_ge(x_loaded.sem, 32)
            norm_total(0, 0, 0)
            for g in range(ADA_FIRST):
                pe.wait_ge(ada_first_summed.sem, g + 1)
                for m in range(DK):
                    col = g * DK + m
                    mm = nc.tensor.matmul(ps[7][:, col:col + 1], ada_total[g][:, P * m:P * m + P], ones[:, 0:1],
                                          start=True, stop=True)
            mm.then_inc(ada_first_ready.sem, 1)

            with loop(ENG.PE, 0, LAYERS) as l:
                ffn(l, 0, 0, C_FFN1)
                pe.wait_ge(mods_done.sem, mods_done(l, HALVES))
                out_product(l, 0, C_FFN1_OUT, UNITS, act_ready, 0, act_hi, act_lo)

                def proj(j, c, c_static, phase, time):
                    b, slot = j % 4, c_static % SLOTS
                    pe.wait_ge(bank[b].sem, bank[b].before(l, phase, time))
                    pe.wait_ge(split.sem, split(l, c + 1))
                    for k in range(DK):
                        mm = product(ps[b][:], slot, k, h_hi[:, k, :], h_lo[:, k, :], k == 0, k == DK - 1)
                    mm.then_inc(used.sem, 1)

                first_four(l, 1, C_PROJ, "proj")
                with loop(ENG.PE, 1, 5) as u:
                    for j in range(4):
                        proj(j, u * 4 + (C_PROJ + j), C_PROJ + j, "proj", u)

                def head_norm(n):
                    b = NORM_BANK[n]
                    pe.wait_ge(bank[b].sem, bank[b].before(l, f"norm{n}"))
                    pe.wait_ge(qk_square.sem, qk_square(l, n + 1))
                    nc.tensor.matmul(ps[b][:], head_ones, tmp[n % 2][:], start=True, stop=True).then_inc(qk_norm.sem, 1)

                def turn(n):
                    b = ROPE_BANK[n]
                    pe.wait_ge(bank[b].sem, bank[b].before(l, f"rope{n}"))
                    pe.wait_ge(qk_normed.sem, qk_normed(l, n + 1))
                    nc.tensor.matmul(ps[b][:], half_turn, k_pad[:, CHUNK:] if n == 0 else tile(q, n - 1),
                                     start=True, stop=True).then_inc(qk_turned.sem, 1)

                def turn_v():
                    pe.wait_ge(bank[J_V % 4].sem, bank[J_V % 4].after(l, "proj", J_V // 4))
                    for b in (4, 5):
                        pe.wait_ge(bank[b].sem, bank[b].before(l, "v_turn"))
                    for ch in range(NCH):
                        mm = nc.tensor.transpose(ps[4 + ch // 4][:, (ch % 4) * P:(ch % 4 + 1) * P],
                                                 v_pad[:, CHUNK * ch:CHUNK * ch + P], ident)
                    mm.then_inc(v_turned.sem, 1)

                pe.wait_ge(pads_ready.sem, pads_ready(l, 1))
                for j in range(J_K, PROJ_TILES):
                    phase, time = ("proj", j // 4) if j < 28 else ("proj_tail", 0)
                    proj(j, C_PROJ + j, C_PROJ + j, phase, time)
                    if 22 <= j < 27:
                        head_norm(j - 22)
                    if j >= 25:
                        if j == 28:
                            turn_v()
                        if j < 29:
                            turn(j - 25) if j != 28 else turn(3)
                turn(4)

                def gate(c, c_static, b, phase, time=0):
                    pe.wait_ge(bank[b].sem, bank[b].before(l, phase, time))
                    pe.wait_ge(split.sem, split(l, c + 1))
                    for k in range(DK):
                        mm = product(ps[b][:], c_static % SLOTS, k, h_hi[:, k, :], h_lo[:, k, :], k == 0, k == DK - 1)
                    mm.then_inc(used.sem, 1)

                def pool_branch(half):
                    c = C_POOL + 5 * half
                    for i in range(4):
                        if half == 1 and i == 1:
                            channel_sum(3, ln_sum, 3, ln_mean)
                        if half == 1 and i == 3:
                            channel_sum(4, xc_summed, 4, ln_var)
                            pe.wait_ge(xc_ready.sem, xc_ready(l, 4))
                        gate(c + i, c + i, i, f"pool{half}")
                    pe.wait_ge(pool_ready.sem, pool_ready(l, 2 * half + 2))
                    pe.wait_ge(split.sem, split(l, c + 5))
                    for i in range(4):
                        b, g = 4 + i, 2 * half + i // 2
                        pe.wait_ge(bank[b].sem, bank[b].before(l, f"pool{half}"))
                        if half == 1 and i == 0:
                            pe.wait_ge(ln_rms.sem, ln_rms(l, 1))
                        mm = product(ps[b][:], (c + 4) % SLOTS, i, pool_hi[:, g, :], pool_lo[:, g, :], True, True)
                    mm.then_inc(used.sem, 1)

                def channel_sum(b, ready, n, done):
                    pe.wait_ge(bank[b].sem, bank[b].before(l, "pool1"))
                    pe.wait_ge(ready.sem, ready(l, n))
                    nc.tensor.matmul(ps[b][:], ones, pair[1][:], start=True, stop=True).then_inc(done.sem, 1)

                pool_branch(0)
                pool_branch(1)

                def own(c, c_static, b, phase, time, rhs_hi, rhs_lo):
                    pe.wait_ge(bank[b].sem, bank[b].before(l, phase, time))
                    pe.wait_ge(split.sem, split(l, c + 1))
                    for k in range(4):
                        mm = product(ps[b][:], c_static % SLOTS, k, rhs_hi[:, k, :], rhs_lo[:, k, :], k == 0, k == 3)
                    mm.then_inc(used.sem, 1)

                def scores(p):
                    pe.wait_ge(q_now_ready.sem, q_now_ready(l, p + 1))
                    for b in (4, 5):
                        pe.wait_ge(bank[b].sem, bank[b].before(l, "sc", p))
                    carry_waits()
                    for ch in range(NCH):
                        for g in range(2):
                            rows = slice(HD * g, HD * g + HD)
                            mm = nc.tensor.matmul(ps[4 + ch // 4][rows, (ch % 4) * P:(ch % 4 + 1) * P],
                                                  q_now[rows, CHUNK * ch:CHUNK * ch + CHUNK],
                                                  k_pad[rows, CHUNK * ch:CHUNK * ch + P], start=True, stop=True)
                    mm.then_inc(scores_ready.sem, 1)

                def turn_probs(p):
                    pe.wait_ge(probs_ready.sem, probs_ready(l, p + 1))
                    for b in (6, 7):
                        pe.wait_ge(bank[b].sem, bank[b].before(l, "sc", p))
                    for ch in range(NCH):
                        mm = nc.tensor.transpose(ps[6 + ch // 4][:, (ch % 4) * P:(ch % 4 + 1) * P],
                                                 probs[:, ch, :], ident)
                    mm.then_inc(probs_turned.sem, 1)

                pe.wait_ge(sc_ready.sem, sc_ready(l, 4))
                pe.wait_ge(qk_ready.sem, qk_ready(l, 5))
                pe.wait_ge(k_first.sem, k_first(l, 1))
                carry_waits()
                with loop(ENG.PE, 0, 4) as p:
                    c = p * 4 + C_SC
                    gate(c, C_SC, 0, "sc", p)
                    scores(p)
                    own(c + 1, C_SC + 1, 1, "sc", p, sc_hi, sc_lo)
                    gate(c + 2, C_SC + 2, 2, "sc", p)
                    own(c + 3, C_SC + 3, 3, "sc", p, sc_hi, sc_lo)
                    turn_probs(p)
                for b in (4, 5, 6, 7):
                    pe.wait_ge(bank[b].sem, bank[b].before(l, "pv"))
                for ch in range(NCH):
                    for g in range(2):
                        cols = (ch % 2) * QT * CHUNK
                        mm = nc.tensor.matmul(ps[4 + ch // 2][HD * g:HD * g + HD, cols:cols + QT * CHUNK],
                                              v_tok[:, ch, HD * g:HD * g + HD],
                                              probs_t[:, ch, g, :, :].rearrange("p i t -> p (i t)"),
                                              start=True, stop=True)
                mm.then_inc(pv_ready.sem, 1)

                def branch(name, c0, rhs_hi, rhs_lo):
                    with loop(ENG.PE, 0, 4) as p:
                        for e in range(2):
                            c = p * 4 + (c0 + 2 * e)
                            gate(c, c0 + 2 * e, 2 * e, name, p)
                            own(c + 1, c0 + 2 * e + 1, 2 * e + 1, name, p, rhs_hi, rhs_lo)

                pe.wait_ge(conv_ready.sem, conv_ready(l, 4))
                carry_waits()
                branch("conv", C_CONV, conv_hi, conv_lo)
                for b in (4, 5, 6, 7):
                    pe.wait_ge(bank[b].sem, bank[b].after(l, "pv"))
                carry_waits()
                branch("attn", C_ATTN, o_hi, o_lo)
                out_product(l, 1, C_WO, DK // 2, mixed_ready, 0, mixed_hi, mixed_lo)
                ffn(l, 1, 2, C_FFN2)
                out_product(l, 2, C_FFN2_OUT, UNITS, act_ready, FK, act_hi, act_lo)


def _lay_out(inputs):
    f = {k: np.asarray(v) for k, v in inputs.items()}
    heads = [h for i in range(QT) for h in (i, i + QT)]

    def in_chunk(w, m):
        return w[:, m * P:m * P + P].reshape(-1, P, P).transpose(1, 0, 2)

    def out_chunk(w, half, c):
        return w.reshape(-1, P, 2, 4, P)[2 * c:2 * c + 2, :, half].transpose(1, 0, 2, 3).reshape(P, 8, P)

    def ffn_chunks(wi, wo):
        for n in range(FK):
            yield in_chunk(wi, n)
            yield in_chunk(wi, FK + n)
        for half in range(2):
            for c in range(FK // 2):
                yield out_chunk(wo, half, c)

    full, half, par = [], [], []
    for l in range(LAYERS):
        full += ffn_chunks(f["ffn1_wi"][l], f["ffn1_wo"][l])
        w = f["w_in"][l]
        cuts = np.cumsum([512, 128, 128, 512, 512, 512, 512, 512])
        wq, wk, wv, wu, wa, wg, wb, wc, wx = np.split(w, cuts, axis=1)
        wq = wq.reshape(D, 8, HD)[:, heads].reshape(D, 512)
        for i in range(4):
            full += [in_chunk(t, i) for t in (wa, wg, wc, wx, wb)]
        full += [in_chunk(wk, 0)] + [in_chunk(wq, i) for i in range(4)] + [in_chunk(wv, 0)]
        full += [in_chunk(wu, i) for i in range(4)]
        gates = [f["w_gate"][l][:, b * D:b * D + D] for b in range(4)]
        for hf in range(2):
            ms = range(4 * hf, 4 * hf + 4)
            half.append(np.stack([f["pool_w"][l, m // 2][:, (m % 2) * P:(m % 2) * P + P] for m in ms], axis=1))
            full += [in_chunk(gates[1], m) for m in ms]
        attn_wo = f["attn_wo"][l].reshape(8, HD, D)[heads].reshape(512, D)
        for b, own in ((3, f["sc_wo"][l]), (2, f["conv_wo"][l]), (0, attn_wo)):
            for m in range(DK):
                full.append(in_chunk(gates[b], m))
                half.append(in_chunk(own, m))
        full += [out_chunk(f["w_o"][l], hf, c) for hf in range(2) for c in range(4)]
        full += ffn_chunks(f["ffn2_wi"][l], f["ffn2_wo"][l])

        def cols(a):
            return a.reshape(-1, P).T

        sinks = f["attn_sinks"][l]
        par.append(np.concatenate([
            cols(f["ffn1_norm"][l]), cols(f["mix_norm"][l]), cols(f["ffn2_norm"][l]), cols(f["b_gate"][l]),
            cols(f["pool_scale"][l]),
            f["conv_dw"][l].reshape(TAPS, 4, P).transpose(2, 1, 0).reshape(P, 4 * TAPS), cols(f["conv_db"][l]),
            cols(f["conv_ln_g"][l]), cols(f["conv_ln_b"][l]),
            f["sc_w"][l].reshape(SC_TAPS, 4, P).transpose(2, 1, 0).reshape(P, 4 * SC_TAPS),
            np.tile(f["q_norm"][l], 2)[:, None], np.tile(f["k_norm"][l], 2)[:, None],
            np.repeat(sinks.reshape(2, QT), HD, axis=0)], axis=1))
    out = {"full": np.stack(full), "half": np.stack(half), "par": np.stack(par)}
    assert out["full"].shape[0] == LAYERS * N_FULL and out["half"].shape[0] == LAYERS * N_HALF

    ada = f["ada_w"].reshape(LAYERS, DK, P, MODS, D).transpose(0, 3, 2, 1, 4).reshape(LAYERS * MODS, P, DK, D)
    spare = ADA_GROUPS - LAYERS * MODS
    out["ada_first"] = ada[:ADA_FIRST].reshape(ADA_FIRST, P, DK // 2, 2, D).transpose(0, 2, 1, 3, 4)
    rest = np.concatenate([ada[ADA_FIRST:], np.zeros((spare, P, DK, D), ada.dtype)])
    out["ada_rest"] = rest.reshape(-1, P, PIECES, 2, 2, T).transpose(0, 4, 2, 1, 3, 5).reshape(-1, P, 2, T)
    ada_b = np.concatenate([f["ada_b"].reshape(-1), np.zeros(spare * D, ada.dtype)]).reshape(-1, P).T
    freq = (10000.0 ** (-np.arange(0, HD, 2, dtype=np.float32) / HD)).astype(np.float32)
    count = np.stack([w / np.minimum(np.arange(1, UPAD + 1), w) for w in WINDOWS]).astype(np.float32).reshape(1, -1)
    out["glob"] = np.concatenate([ada_b, f["c"].reshape(DK, P).T, np.tile(freq, 4)[:, None],
                                  np.repeat(count, P, axis=0)], axis=1)
    out["positions"] = np.broadcast_to(f["positions"].reshape(1, T), (P, T))
    out["x"] = f["x"].reshape(T, DK, P).transpose(2, 1, 0)
    i = np.arange(P)
    turn = np.zeros((P, P), np.float32)
    low = i[i % HD < HD // 2]
    turn[low + HD // 2, low] = -1.0
    turn[low, low + HD // 2] = 1.0
    out["mats"] = np.stack([np.ones((P, P), np.float32), (i[:, None] // HD == i // HD).astype(np.float32), turn,
                            np.eye(P, dtype=np.float32)], axis=1)
    return {k: np.ascontiguousarray(v) for k, v in out.items()}


def kernel(**inputs):
    import concourse.bacc as bacc
    from concourse.bass_utils import run_bass_kernel_spmd

    arrays = _lay_out(inputs)
    nc = bacc.Bacc("TRN2", target_bir_lowering=False, num_devices=1)
    io = {name: nc.dram_tensor(name + "_in", a.shape, mybir.dt.from_np(a.dtype), kind="ExternalInput").ap()
          for name, a in arrays.items()}
    io["rope_scratch"] = nc.dram_tensor("rope_scratch", (P, 2, T), F32).ap()
    io["out"] = nc.dram_tensor("out_x", (P, DK, T), F32, kind="ExternalOutput").ap()
    trunk_program(nc, io)
    r = run_bass_kernel_spmd(nc, [{name + "_in": a for name, a in arrays.items()}], core_ids=[0])
    return r.results[0]["out_x"].transpose(2, 1, 0).reshape(1, T, D)
```
